# Optimizing a Trainium2 kernel written in Bass

```python
import math
import jax, jax.numpy as jnp
from jax import lax
import numpy as np

D_MODEL = 1024
BATCH = 1
SEQ = 1024
DEPTH = 1

CHUNK = 64
D_MIX = D_MODEL
POOL_WIDTH = D_MIX // 2
POOL_WINDOWS = (2, 4, 8, 16)
POOL_GROUPS = len(POOL_WINDOWS)
POOL_CH = POOL_WIDTH // POOL_GROUPS
HEAD_DIM = 64
N_Q_HEADS = (D_MIX - POOL_WIDTH) // HEAD_DIM
N_KV_HEADS = 2
Q_PER_KV = N_Q_HEADS // N_KV_HEADS
WINDOW = 128
N_WIN_CHUNKS = WINDOW // CHUNK
D_FF = 4 * D_MODEL
Q_WIDTH = N_Q_HEADS * HEAD_DIM
KV_WIDTH = N_KV_HEADS * HEAD_DIM
IN_WIDTH = POOL_WIDTH + Q_WIDTH + 2 * KV_WIDTH
NORM_EPS = 1e-6
MASK_VALUE = -1e30

kernel_name = "hybrid_pool_swa_sink_alibi_trunk"

def rms_norm(x, g):
    xf = x.astype(jnp.float32)
    y = xf * lax.rsqrt(jnp.mean(xf * xf, axis=-1, keepdims=True) + NORM_EPS)
    return (y * g.astype(jnp.float32)).astype(x.dtype)

def alibi_slopes(n_heads):
    return jnp.asarray([2.0 ** (-8.0 * (h + 1) / n_heads) for h in range(n_heads)], dtype=jnp.float32)

def pool_mixer(u, pool_w, pool_scale):
    B, S, _ = u.shape
    ug = u.reshape(B, S, POOL_GROUPS, POOL_CH).astype(jnp.float32)
    cs = jnp.pad(jnp.cumsum(ug, axis=1), ((0, 0), (1, 0), (0, 0), (0, 0)))
    t = jnp.arange(S)
    outs = []
    for g, w in enumerate(POOL_WINDOWS):
        csg = cs[:, :, g]
        lo = jnp.maximum(t + 1 - w, 0)
        win_sum = csg[:, t + 1] - csg[:, lo]
        count = jnp.minimum(t + 1, w).astype(jnp.float32)[None, :, None]
        outs.append(win_sum / count - ug[:, :, g])
    pooled = jnp.stack(outs, axis=2).astype(u.dtype)
    mixed = jnp.einsum('bsgc,gcd->bsgd', pooled, pool_w)
    return mixed.reshape(B, S, POOL_WIDTH) * pool_scale

def swa_sink_attention(q, k, v, q_norm_g, k_norm_g, sinks):
    B, S = q.shape[:2]
    NC = S // CHUNK
    q = rms_norm(q, q_norm_g)
    k = rms_norm(k, k_norm_g)
    qc = q.reshape(B, NC, CHUNK, N_KV_HEADS, Q_PER_KV, HEAD_DIM)
    kc = k.reshape(B, NC, CHUNK, N_KV_HEADS, HEAD_DIM)
    vc = v.reshape(B, NC, CHUNK, N_KV_HEADS, HEAD_DIM)

    def band(xc):
        shifted = []
        for r in range(N_WIN_CHUNKS - 1, -1, -1):
            shifted.append(jnp.pad(xc, ((0, 0), (r, 0), (0, 0), (0, 0), (0, 0)))[:, :NC])
        return jnp.concatenate(shifted, axis=2)

    kb, vb = band(kc), band(vc)
    KL = N_WIN_CHUNKS * CHUNK
    s = jnp.einsum('bnikgd,bnjkd->bnkgij', qc, kb,
                   preferred_element_type=jnp.float32) * (1.0 / math.sqrt(HEAD_DIM))
    i_pos = jnp.arange(CHUNK)[:, None] + (N_WIN_CHUNKS - 1) * CHUNK
    j_pos = jnp.arange(KL)[None, :]
    dist = jnp.abs(i_pos - j_pos).astype(jnp.float32)
    slopes = alibi_slopes(N_Q_HEADS).reshape(N_KV_HEADS, Q_PER_KV)
    s = s - slopes[:, :, None, None] * dist
    key_chunk = jnp.arange(NC)[:, None] - (N_WIN_CHUNKS - 1) + jnp.arange(KL)[None, :] // CHUNK
    valid = key_chunk >= 0
    s = jnp.where(valid[None, :, None, None, None, :], s, MASK_VALUE)
    sink = sinks.astype(jnp.float32).reshape(N_KV_HEADS, Q_PER_KV)[None, None, :, :, None, None]
    m = jnp.maximum(jnp.max(s, axis=-1, keepdims=True), sink)
    p = jnp.exp(s - m)
    p = p / (jnp.sum(p, axis=-1, keepdims=True) + jnp.exp(sink - m))
    o = jnp.einsum('bnkgij,bnjkd->bnikgd', p.astype(vb.dtype), vb)
    return o.reshape(B, S, Q_WIDTH)

def setup_inputs(seed: int = 0) -> dict:
    key = jax.random.key(seed)
    ks = jax.random.split(key, 12)
    f32 = jnp.float32
    x = jax.random.normal(ks[0], (BATCH, SEQ, D_MODEL), f32)
    norm1_g = 1.0 + 0.05 * jax.random.normal(ks[1], (DEPTH, D_MODEL), f32)
    w_in = jax.random.normal(ks[2], (DEPTH, D_MODEL, IN_WIDTH), f32) * D_MODEL ** -0.5
    pool_w = jax.random.normal(ks[3], (DEPTH, POOL_GROUPS, POOL_CH, POOL_CH), f32) * POOL_CH ** -0.5
    pool_scale = 1.0 + 0.1 * jax.random.normal(ks[4], (DEPTH, POOL_WIDTH), f32)
    q_norm_g = 1.0 + 0.05 * jax.random.normal(ks[5], (DEPTH, HEAD_DIM), f32)
    k_norm_g = 1.0 + 0.05 * jax.random.normal(ks[6], (DEPTH, HEAD_DIM), f32)
    sinks = 0.5 * jax.random.normal(ks[7], (DEPTH, N_Q_HEADS), f32)
    w_out = jax.random.normal(ks[8], (DEPTH, D_MIX, D_MODEL), f32) * D_MIX ** -0.5
    norm2_g = 1.0 + 0.05 * jax.random.normal(ks[9], (DEPTH, D_MODEL), f32)
    w_up = jax.random.normal(ks[10], (DEPTH, D_MODEL, D_FF), f32) * D_MODEL ** -0.5
    w_down = jax.random.normal(ks[11], (DEPTH, D_FF, D_MODEL), f32) * D_FF ** -0.5
    return {"x": x, "norm1_g": norm1_g, "w_in": w_in, "pool_w": pool_w,
            "pool_scale": pool_scale, "q_norm_g": q_norm_g, "k_norm_g": k_norm_g,
            "sinks": sinks, "w_out": w_out, "norm2_g": norm2_g,
            "w_up": w_up, "w_down": w_down}

def reference(x, norm1_g, w_in, pool_w, pool_scale, q_norm_g, k_norm_g, sinks,
              w_out, norm2_g, w_up, w_down):
    B, S, _ = x.shape
    for l in range(DEPTH):
        h = rms_norm(x, norm1_g[l])
        proj = jnp.einsum('bsd,de->bse', h, w_in[l])
        u = proj[..., :POOL_WIDTH]
        q = proj[..., POOL_WIDTH:POOL_WIDTH + Q_WIDTH].reshape(B, S, N_Q_HEADS, HEAD_DIM)
        k = proj[..., POOL_WIDTH + Q_WIDTH:POOL_WIDTH + Q_WIDTH + KV_WIDTH].reshape(B, S, N_KV_HEADS, HEAD_DIM)
        v = proj[..., POOL_WIDTH + Q_WIDTH + KV_WIDTH:].reshape(B, S, N_KV_HEADS, HEAD_DIM)
        a = pool_mixer(u, pool_w[l], pool_scale[l])
        b = swa_sink_attention(q, k, v, q_norm_g[l], k_norm_g[l], sinks[l])
        x = x + jnp.einsum('bse,ed->bsd', jnp.concatenate([a, b], axis=-1), w_out[l])
        h2 = rms_norm(x, norm2_g[l])
        hid = jnp.square(jax.nn.relu(jnp.einsum('bsd,df->bsf', h2, w_up[l])))
        x = x + jnp.einsum('bsf,fd->bsd', hid, w_down[l])
    return x


_drawn_inputs = setup_inputs


def setup_inputs(seed=0):
    import zlib

    import numpy as np

    out = dict(_drawn_inputs(seed))
    spreads = {}
    factors = {'q_norm_g': 7.525, 'k_norm_g': 7.373, 'sinks': 8.0}
    for name, (base, spread) in spreads.items():
        noise = np.random.default_rng([zlib.crc32(name.encode()), seed]).standard_normal(out[name].shape)
        drawn = base * np.exp(spread * noise) if base else spread * noise
        out[name] = __import__('jax').numpy.asarray(drawn.astype(out[name].dtype))
    for name, factor in factors.items():
        out[name] = (out[name] * factor).astype(out[name].dtype)
    return out
```

```python
import concourse.bass as bass
from concourse import mybir
from contextlib import ExitStack

F32 = mybir.dt.float32
F32R = mybir.dt.float32r
BF16 = mybir.dt.bfloat16
ALU = mybir.AluOpType
ACT = mybir.ActivationFunctionType
AX = mybir.AxisListType

P = 128
BANK = 512
HI, LO = 0, 1


def hybrid_trunk(nc, x, norm1_g, w_in, pool_w, pool_scale, q_norm_g, k_norm_g, sinks,
                 w_out, norm2_g, w_up, w_down, out):
    SEQ, D = x.shape[1], x.shape[2]
    IN_W = w_in.shape[2]
    GROUPS = pool_w.shape[1]
    POOL_W = pool_scale.shape[1]
    HD = q_norm_g.shape[1]
    NQ = sinks.shape[1]
    D_FF = w_up.shape[2]
    CHUNK = HD
    Q_W = NQ * HD
    KT = D // P
    NT = SEQ // P
    NCH = 2 * NT
    PAIRS = NQ // 2
    WINDOWS = [2 << g for g in range(GROUPS)]
    HALO = WINDOWS[-1]
    EPS = 1e-6
    MASK = -1e30
    FC = 4
    CH_FF = FC * P
    NC_FF = D_FF // CH_FF
    assert KT == 8 and NT == 8 and PAIRS == 4 and IN_W == POOL_W + Q_W + 2 * P and D == 2 * BANK

    x_t = x[0].rearrange("(t p) d -> t p d", p=P)
    out_t = out[0].rearrange("(t p) d -> t p d", p=P)
    w_in_k = w_in[0].rearrange("(k p) e -> k p e", p=P)
    w_out_k = w_out[0].rearrange("(k p) n -> k p n", p=P)
    w_up_k = w_up[0].rearrange("(k p) f -> p k f", p=P)
    w_down_c = w_down[0].rearrange("(c f p) n -> c p f n", p=P, f=FC)
    pool_w_g = pool_w[0].rearrange("g c d -> c g d")

    with ExitStack() as ctx:
        def sem(name):
            return ctx.enter_context(nc.semaphore(name))

        act = ctx.enter_context(nc.sbuf_tensor("act", [P, 2, KT, SEQ], F32R))
        act_f = act[:, :, :, :].bitcast(F32)
        WGT = 2 * KT * IN_W
        wgt = ctx.enter_context(nc.sbuf_tensor("wgt", [P, WGT], F32R))
        w_in_s = wgt[:, :].rearrange("p (k h e) -> p k h e", k=KT, h=2)
        w_out_s = wgt[:, 0:2 * KT * D].rearrange("p (k h n) -> p k h n", k=KT, h=2)
        hid = wgt[:, 0:2 * FC * SEQ].rearrange("p (f h s) -> p f h s", f=FC, h=2)
        DN0 = 2 * FC * SEQ
        DNW = 2 * FC * BANK
        down_s = [wgt[:, DN0 + i * DNW:DN0 + (i + 1) * DNW].rearrange("p (h f n) -> p h f n", h=2, f=FC)
                  for i in range(2)]
        UP0 = DN0 + 2 * DNW
        UPW = 2 * KT * P
        up_s = [wgt[:, UP0 + i * UPW:UP0 + (i + 1) * UPW].rearrange("p (h k n) -> p h k n", h=2, k=KT)
                for i in range(2)]
        assert UP0 + 2 * UPW <= WGT

        FREE = 16336
        mem = ctx.enter_context(nc.sbuf_tensor("mem", [P, FREE], F32))
        at = [0]

        def take(words):
            a = at[0]
            at[0] += words
            assert at[0] <= FREE
            return a

        def view(a, words):
            return mem[:, a:a + words]

        KV_W = 2 * P
        UB = HALO + P
        a_x = take(2 * D)
        a_A = take(2 * D)
        a_B = take(4 * D)
        a_C = take(3 * D)
        a_ws = take(2 * D)
        a_xn = take(D)
        a_bp = take(D)
        a_junk = take(D // 2)
        x_slot = [view(a_x + i * D, D) for i in range(2)]
        u_tok = view(a_A, POOL_W)
        qkv = view(a_A + POOL_W, Q_W + KV_W)
        squares = view(a_A + POOL_W + Q_W + KV_W, Q_W + P)
        b = a_B
        keys_T = view(b, CHUNK + SEQ); b += CHUNK + SEQ
        q_diag = view(b, 2 * PAIRS * P).rearrange("p (c t n) -> p c t n", c=2, t=PAIRS); b += 2 * PAIRS * P
        u_T = view(b, GROUPS * UB).rearrange("p (g s) -> p g s", g=GROUPS); b += GROUPS * UB
        win_a = view(b, GROUPS * UB).rearrange("p (g s) -> p g s", g=GROUPS); b += GROUPS * UB
        win_b = view(b, 3 * UB).rearrange("p (g s) -> p g s", g=3); b += 3 * UB
        assert b <= a_B + 4 * D
        scores = [view(a_C + i * BANK, BANK).rearrange("p (t j) -> p t j", t=PAIRS) for i in range(2)]
        probs_T = [view(a_C + D + i * BANK, BANK) for i in range(2)]
        values = view(a_C + 2 * D, 8 * P).rearrange("p (r c n) -> p r c n", r=4, c=2)
        x_norm = view(a_xn, D)
        bias = view(a_bp, BANK).rearrange("p (t j) -> p t j", t=PAIRS)
        pool_map = view(a_bp + BANK, BANK).rearrange("p (g n) -> p g n", g=GROUPS)
        junk = view(a_junk, D // 2).bitcast(BF16)
        w_in_stage = ([view(a_C + i * IN_W, IN_W) for i in range(2)] + [view(a_A, IN_W)]
                      + [view(a_B + i * IN_W, IN_W) for i in range(3)])
        w_out_stage = [view(a, D) for a in (a_ws, a_ws + D, a_x, a_x + D, a_xn)]
        W_OUT_SLOT = [0, 1, 2, 3, 4, 0, 1, 4]
        dist = view(a_ws, P)
        resid = ([view(a_x + i * D, D) for i in range(2)] + [view(a_A + i * D, D) for i in range(2)]
                 + [view(a_B + i * D, D) for i in range(4)])
        norm2_row = view(a_bp, D)
        up_stage = [view(a_C + i * D, D).rearrange("p (k n) -> p k n", k=KT) for i in range(2)]
        relu_buf = [view(a_C + 2 * D + i * BANK, BANK) for i in range(2)]
        down_stage = [view(a_ws, 2 * D).rearrange("p (f n) -> p f n", f=FC),
                      view(a_xn, 2 * D).rearrange("p (f n) -> p f n", f=FC)]
        ident = view(take(P), P)
        small = lambda n: view(take(n), n)
        g1 = small(KT)
        q_gain, k_gain = small(1), small(1)
        neg_sink = small(PAIRS)
        pool_sc = small(GROUPS)
        minus_half = small(10)
        edge = small(GROUPS * HALO).rearrange("p (g j) -> p g j", g=GROUPS)
        NH = NQ + 2
        ssq, var, rinv = small(2 * NT), small(2 * NT), small(2 * NT)
        h_ssq, h_var, h_rinv = small(NH), small(NH), small(NH)
        pair = lambda: [small(PAIRS) for _ in range(2)]
        smax, neg_max, sink_gap, sink_exp, row_sum, denom, inv_den = (pair() for _ in range(7))

        bank = [ctx.enter_context(nc.psum_tensor(f"bank{i}", [P, BANK], F32)) for i in range(8)]
        KV_B, Q_B, U_B = 2, 3, 4
        XT_B = [[0, 1], [5, 6]]
        UT_B, QT_B, KT_B = 0, 1, 7
        MIX_B, SC_B, OUT_B = 0, [5, 6], [7, 1]
        TOK_B = [2, 3, 4, 0]
        Z_B = [1, 7]

        gain1_in, consts_in = sem("gain1_in"), sem("consts_in")
        x_in = [sem(f"x_in{i}") for i in range(2)]
        resid_in = [sem(f"resid_in{i}") for i in range(NT)]
        norm2_in = sem("norm2_in")
        w_in_in = [sem(f"w_in_in{i}") for i in range(6)]
        w_out_in = [sem(f"w_out_in{i}") for i in range(5)]
        up_in = [sem(f"up_in{i}") for i in range(2)]
        down_in = [sem(f"down_in{i}") for i in range(2)]
        stored = sem("stored")
        zeroed, setup_pool, setup_dve, setup_done = sem("zeroed"), sem("setup_pool"), sem("setup_dve"), sem("setup_done")
        pads_ready = sem("pads_ready")
        sumsq_ready, var_ready, rinv_ready, x_norm_ready = sem("sumsq_ready"), sem("var_ready"), sem("rinv_ready"), sem("x_norm_ready")
        xT_done, xT_hi, xT_lo = sem("xT_done"), sem("xT_hi"), sem("xT_lo")
        w_in_hi, w_in_lo = sem("w_in_hi"), sem("w_in_lo")
        rows_hi, rows_lo = sem("rows_hi"), sem("rows_lo")
        up_hi, up_lo = sem("up_hi"), sem("up_lo")
        in_done = sem("in_done")
        kv_copied, q_copied, u_copied = sem("kv_copied"), sem("q_copied"), sem("u_copied")
        squares_ready, h_ssq_ready, h_var_ready, h_rinv_ready, qk_ready = (sem(n) for n in (
            "squares_ready", "h_ssq_ready", "h_var_ready", "h_rinv_ready", "qk_ready"))
        values_ready = sem("values_ready")
        uT_done, qT_done, kT_done = sem("uT_done"), sem("qT_done"), sem("kT_done")
        halo_ready, u_T_ready, q_diag_ready, keys_ready = sem("halo_ready"), sem("u_T_ready"), sem("q_diag_ready"), sem("keys_ready")
        win_step, windows_ready, pool_step, pooled_ready = sem("win_step"), sem("windows_ready"), sem("pool_step"), sem("pooled_ready")
        mix_done, mix_hi, mix_lo = sem("mix_done"), sem("mix_hi"), sem("mix_lo")
        scores_done, biased, max_ready, negmax_ready, gap_ready = (sem(n) for n in (
            "scores_done", "biased", "max_ready", "negmax_ready", "gap_ready"))
        exp_done, denom_ready, inv_ready, probs_ready = (sem(n) for n in (
            "exp_done", "denom_ready", "inv_ready", "probs_ready"))
        pT_done, pT_copied, pv_done, att_hi, att_lo = (sem(n) for n in (
            "pT_done", "pT_copied", "pv_done", "att_hi", "att_lo"))
        tok_done, tok_added = sem("tok_done"), sem("tok_added")
        z_done, relu_done, sq_done, hid_hi, hid_lo = (sem(n) for n in (
            "z_done", "relu_done", "sq_done", "hid_hi", "hid_lo"))

        N_CONST = 7 + GROUPS
        HALF = SEQ // 2
        ORDER = [(2 * p + i, h) for p in range(FC // 2) for h in range(2) for i in range(2)]
        NZ = len(ORDER)
        NTOK = 2 * NT

        def tile(t):
            return slice(t * P, (t + 1) * P)

        block = ctx.enter_context(nc.Block())

        @block.sync
        def _(sp):
            def load_x(t):
                if t >= 2:
                    sp.wait_ge(x_norm_ready, t - 1)
                sp.dma_start(x_slot[t % 2], x_t[t]).then_inc(x_in[t % 2], 16)

            def load_w_in(k):
                if k >= 6:
                    sp.wait_ge(w_in_lo, k - 5)
                sp.dma_start(w_in_stage[k % 6], w_in_k[k]).then_inc(w_in_in[k % 6], 16)

            def load_w_out(k):
                slot = W_OUT_SLOT[k]
                if slot in W_OUT_SLOT[:k]:
                    sp.wait_ge(rows_lo, W_OUT_SLOT.index(slot) + 1)
                dst, done = w_out_stage[slot], w_out_in[slot]
                if k < KT // 2:
                    sp.dma_start(dst, w_out_k[k]).then_inc(done, 16)
                else:
                    for s in range(2):
                        r = POOL_W + (s * PAIRS + k - KT // 2) * HD
                        sp.dma_start(dst[s * HD:(s + 1) * HD, :], w_out[0, r:r + HD, :]).then_inc(done, 16)

            def load_up(slot, c, f):
                sp.dma_start(up_stage[slot], w_up_k[:, :, bass.ds(c * CH_FF + f * P, P)]).then_inc(up_in[slot], 16)

            def load_down(c, dh):
                sp.dma_start(down_stage[dh], w_down_c[c, :, :, dh * BANK:(dh + 1) * BANK]).then_inc(down_in[dh], 16)

            load_x(0)
            for k in range(4):
                load_w_in(k)
            load_x(1)
            for k in range(4, KT):
                load_w_in(k)
            for t in range(2, NT):
                load_x(t)
            sp.wait_ge(setup_done, 1)
            load_w_out(0)
            load_w_out(1)
            sp.wait_ge(x_norm_ready, NT - 1)
            load_w_out(2)
            sp.wait_ge(x_norm_ready, NT)
            load_w_out(3)
            sp.wait_ge(xT_done, 2 * NT)
            load_w_out(4)
            for k in range(5, KT):
                load_w_out(k)
            sp.wait_ge(rows_lo, 4)
            for t in range(2):
                sp.dma_start(resid[t], x_t[t]).then_inc(resid_in[t], 16)
            sp.wait_ge(uT_done, NT)
            sp.wait_ge(kT_done, NT)
            sp.wait_ge(values_ready, NT)
            for t in range(2, 4):
                sp.dma_start(resid[t], x_t[t]).then_inc(resid_in[t], 16)
            sp.wait_ge(mix_done, NT)
            sp.wait_ge(scores_done, NCH)
            sp.wait_ge(biased, NCH)
            sp.dma_start(norm2_row, norm2_g.to_broadcast([P, D])).then_inc(norm2_in, 16)
            for t in range(4, NT):
                sp.dma_start(resid[t], x_t[t]).then_inc(resid_in[t], 16)
            sp.wait_ge(pv_done, NCH)
            load_up(0, 0, 0)
            load_up(1, 0, 1)

            def chunk(c, first=False, last=False):
                U = c * FC
                sp.wait_ge(up_lo, U + 1)
                load_up(0, c, 2)
                sp.wait_ge(up_lo, U + 2)
                load_up(1, c, 3)
                if first:
                    sp.wait_ge(xT_done, 4 * NT)
                sp.wait_ge(rows_lo, c * 2 + KT - 1)
                load_down(c, 0)
                sp.wait_ge(rows_lo, c * 2 + KT)
                load_down(c, 1)
                if not last:
                    sp.wait_ge(up_lo, U + 3)
                    load_up(0, c + 1, 0)
                    sp.wait_ge(up_lo, U + 4)
                    load_up(1, c + 1, 1)

            chunk(0, first=True)
            with sp.Fori(1, NC_FF - 1) as c:
                chunk(c)
            chunk(NC_FF - 1, last=True)
            for g in range(NTOK):
                dh, t = divmod(g, NT)
                sp.wait_ge(tok_added, NTOK * NC_FF + g + 1)
                sp.dma_start(out_t[t][:, dh * BANK:(dh + 1) * BANK],
                             resid[t][:, dh * BANK:(dh + 1) * BANK]).then_inc(stored, 16)
            sp.wait_ge(stored, 16 * NTOK)

        @block.gpsimd
        def _(pool):
            nc.gpsimd.memset(ident, 0.0).then_inc(setup_pool, 1)
            nc.gpsimd.memset(minus_half, -0.5).then_inc(setup_pool, 1)
            pool.wait_ge(setup_pool, 2)
            nc.gpsimd.affine_select(out=ident, in_=ident, compare_op=ALU.not_equal, fill=1.0, base=0,
                                    pattern=[[-1, P]], channel_multiplier=1).then_inc(setup_pool, 1)
            for s in range(2):
                pool.wait_ge(setup_pool, 3 + s)
                nc.gpsimd.iota(dist[s * HD:(s + 1) * HD, :], [[-1, P]], base=CHUNK, channel_multiplier=1,
                               allow_small_or_imprecise_dtypes=True).then_inc(setup_pool, 1)
            pool.wait_ge(setup_pool, 5)
            nc.gpsimd.iota(edge, [[0, GROUPS], [1, HALO]], base=1, channel_multiplier=0,
                           allow_small_or_imprecise_dtypes=True).then_inc(setup_pool, 1)
            pool.wait_ge(setup_pool, 6)

            def inverse_rms(T):
                pool.wait_ge(sumsq_ready, T + 1)
                nc.gpsimd.tensor_scalar(out=var[:, T:T + 1], in0=ssq[:, T:T + 1], scalar1=1.0 / D, scalar2=EPS,
                                        op0=ALU.mult, op1=ALU.add).then_inc(var_ready, 1)
                pool.wait_ge(var_ready, T + 1)
                nc.gpsimd.tensor_tensor(out=rinv[:, T:T + 1], in0=var[:, T:T + 1], in1=minus_half[:, 0:1],
                                        op=ALU.pow).then_inc(rinv_ready, 1)

            def window_sums(t):
                pool.wait_ge(u_T_ready, t + 1)
                if t == 0:
                    pool.wait_ge(pads_ready, 1)
                if t >= 1:
                    pool.wait_ge(mix_done, t)
                sums = [(win_a, 0, u_T, 0, 0, 1), (win_b, 0, win_a, 1, 1, 2),
                        (win_a, 2, win_b, 1, 2, 4), (win_b, 2, win_a, 3, 3, 8)]
                for n, (dst, d0, src, s0, g0, shift) in enumerate(sums):
                    cnt, lo = GROUPS - g0, 2 * shift - 1
                    if n:
                        pool.wait_ge(win_step, 4 * t + n)
                    nc.gpsimd.tensor_tensor(out=dst[:, d0:d0 + cnt, lo:UB], in0=src[:, s0:s0 + cnt, lo:UB],
                                            in1=src[:, s0:s0 + cnt, lo - shift:UB - shift],
                                            op=ALU.add).then_inc(win_step, 1)

            def head_squares(t):
                pool.wait_ge(q_copied, t + 1)
                pool.wait_ge(kv_copied, t + 1)
                qk = qkv[:, 0:Q_W + P]
                nc.gpsimd.tensor_tensor(out=squares, in0=qk, in1=qk, op=ALU.mult).then_inc(squares_ready, 1)

            def head_inverse_rms(t):
                pool.wait_ge(h_ssq_ready, t + 1)
                nc.gpsimd.tensor_scalar(out=h_var, in0=h_ssq, scalar1=1.0 / HD, scalar2=EPS,
                                        op0=ALU.mult, op1=ALU.add).then_inc(h_var_ready, 1)
                pool.wait_ge(h_var_ready, t + 1)
                nc.gpsimd.tensor_tensor(out=h_rinv, in0=h_var, in1=minus_half, op=ALU.pow).then_inc(h_rinv_ready, 1)

            inverse_rms(0)
            inverse_rms(1)
            for t in range(NT + 2):
                if t + 2 < NT:
                    inverse_rms(t + 2)
                if 0 <= t - 1 < NT:
                    window_sums(t - 1)
                if t < NT:
                    head_squares(t)
                    head_inverse_rms(t)
                else:
                    inverse_rms(t)
            for T in range(NT + 2, 2 * NT):
                inverse_rms(T)

        @block.scalar
        def _(sc):
            def sum_squares(T, src):
                nc.scalar.activation(junk, src, ACT.Square, accum_out=ssq[:, T:T + 1]).then_inc(sumsq_ready, 1)

            def sum_squares_x(t):
                sc.wait_ge(x_in[t % 2], 16 * (t // 2 + 1))
                sum_squares(t, x_slot[t % 2])

            def sum_squares_x1(t):
                sc.wait_ge(tok_added, 2 * t + 2)
                sum_squares(NT + t, resid[t])

            def xT_high(T):
                t = T % NT
                for i in range(2):
                    sc.wait_ge(xT_done, 2 * T + i + 1)
                    src = bank[XT_B[T // NT][i]][:, :].rearrange("p (k n) -> p k n", k=4)
                    nc.scalar.activation(act[:, HI, 4 * i:4 * i + 4, tile(t)], src, ACT.Copy).then_inc(xT_hi, 1)

            def split_w_in(k):
                if k == 0:
                    sc.wait_ge(gain1_in, 16)
                sc.wait_ge(w_in_in[k % 6], 16 * (k // 6 + 1))
                nc.scalar.activation(w_in_s[:, k, HI, :], w_in_stage[k % 6], ACT.Copy,
                                     scale=g1[:, k:k + 1]).then_inc(w_in_hi, 1)

            def split_w_out(k):
                sc.wait_ge(in_done, KT * (NT - 1) + (2 * D * (k + 1) - 1) // (2 * IN_W) + 1)
                sc.wait_ge(w_out_in[W_OUT_SLOT[k]], w_out_count(k))
                nc.scalar.activation(w_out_s[:, k, HI, :], w_out_stage[W_OUT_SLOT[k]], ACT.Copy).then_inc(rows_hi, 1)

            def w_out_count(k):
                return sum(16 if j < KT // 2 else 32 for j in range(k + 1) if W_OUT_SLOT[j] == W_OUT_SLOT[k])

            def copy_in(t):
                if t >= 1:
                    sc.wait_ge(values_ready, t)
                    sc.wait_ge(uT_done, t)
                    sc.wait_ge(kT_done, t)
                sc.wait_ge(in_done, KT * (t + 1))
                nc.scalar.activation(qkv[:, Q_W:Q_W + KV_W], bank[KV_B][:, 0:KV_W], ACT.Copy).then_inc(kv_copied, 1)
                nc.scalar.activation(qkv[:, 0:Q_W].rearrange("p (t s d) -> p s t d", s=2, t=PAIRS),
                                     bank[Q_B][:, :].rearrange("p (s t d) -> p s t d", s=2, t=PAIRS),
                                     ACT.Copy).then_inc(q_copied, 1)

            def copy_u(t):
                nc.scalar.activation(u_tok, bank[U_B][:, :], ACT.Copy).then_inc(u_copied, 1)

            def evac_transposed(t):
                if t == 0:
                    sc.wait_ge(pads_ready, 1)
                    sc.wait_ge(setup_done, 1)
                sc.wait_ge(uT_done, t + 1)
                if t >= 1:
                    sc.wait_ge(pooled_ready, t)
                    sc.wait_ge(u_T_ready, t)
                    nc.scalar.activation(u_T[:, :, 0:HALO], u_T[:, :, P:P + HALO], ACT.Copy).then_inc(halo_ready, 1)
                    sc.wait_ge(halo_ready, t)
                nc.scalar.activation(u_T[:, :, HALO:UB], bank[UT_B][:, :].rearrange("p (g n) -> p g n", g=GROUPS),
                                     ACT.Copy).then_inc(u_T_ready, 1)
                sc.wait_ge(qT_done, t + 1)
                src = bank[QT_B][:, :].rearrange("p (t c i) -> p c t i", t=PAIRS, c=2)
                for s in range(2):
                    half = slice(s * HD, (s + 1) * HD)
                    nc.scalar.activation(q_diag[half, :, :, half], src[half, :, :, :], ACT.Copy,
                                         scale=q_gain[half, :]).then_inc(q_diag_ready, 1)
                sc.wait_ge(kT_done, t + 1)
                nc.scalar.activation(keys_T[:, CHUNK + t * P:CHUNK + (t + 1) * P], bank[KT_B][:, 0:P], ACT.Copy,
                                     scale=k_gain).then_inc(keys_ready, 1)

            def evac_probs(t, cs=(0, 1)):
                for c in cs:
                    n = 2 * t + c
                    sc.wait_ge(pT_done, n + 1)
                    if t >= 1:
                        sc.wait_ge(pv_done, n - 1)
                    nc.scalar.activation(probs_T[c], bank[SC_B[c]][:, :], ACT.Copy).then_inc(pT_copied, 1)

            def mix_high(t):
                sc.wait_ge(mix_done, t + 1)
                for g in range(GROUPS):
                    nc.scalar.activation(act[:, HI, g, tile(t)], bank[MIX_B][:, g * P:(g + 1) * P], ACT.Copy,
                                         scale=pool_sc[:, g:g + 1]).then_inc(mix_hi, 1)

            def attention_high(t):
                for c in range(2):
                    n = 2 * t + c
                    sc.wait_ge(pv_done, n + 1)
                    src = bank[OUT_B[c]][:, :].rearrange("p (t s i) -> p s t i", t=PAIRS, s=2)
                    tok = slice(n * CHUNK, (n + 1) * CHUNK)
                    for s in range(2):
                        half = slice(s * HD, (s + 1) * HD)
                        nc.scalar.activation(act[half, HI, 4:8, tok], src[half, s, :, :], ACT.Copy).then_inc(att_hi, 1)

            def exponentials(t):
                for c in range(2):
                    n = 2 * t + c
                    sc.wait_ge(negmax_ready, n + 1)
                    for pr in range(PAIRS):
                        nc.scalar.activation(scores[c][:, pr, :], scores[c][:, pr, :], ACT.Exp,
                                             bias=neg_max[c][:, pr:pr + 1],
                                             accum_out=row_sum[c][:, pr:pr + 1]).then_inc(exp_done, 1)
                    sc.wait_ge(gap_ready, n + 1)
                    nc.scalar.activation(sink_exp[c], sink_gap[c], ACT.Exp).then_inc(exp_done, 1)

            def split_up(slot, U):
                sc.wait_ge(up_in[slot], U * 8 + 16 if slot == 0 else U * 8 + 8)
                nc.scalar.activation(up_s[slot][:, HI, :, :], up_stage[slot], ACT.Copy).then_inc(up_hi, 1)

            def split_down(c, dh):
                sc.wait_ge(down_in[dh], c * 16 + 16)
                nc.scalar.activation(down_s[dh][:, HI, :, :], down_stage[dh], ACT.Copy).then_inc(rows_hi, 1)

            with nc.allow_non_contiguous_dma(reason="small per-partition gains"):
                sc.dma_start(g1, norm1_g[0].rearrange("(k p) -> p k", p=P)).then_inc(gain1_in, 16)
                sc.dma_start(pool_sc, pool_scale[0].rearrange("(g p) -> p g", p=P)).then_inc(consts_in, 16)
                for s in range(2):
                    half = slice(s * HD, (s + 1) * HD)
                    sc.dma_start(q_gain[half, :], q_norm_g[0].rearrange("(p a) -> p a", a=1)).then_inc(consts_in, 16)
                    sc.dma_start(k_gain[half, :], k_norm_g[0].rearrange("(p a) -> p a", a=1)).then_inc(consts_in, 16)
                    sc.dma_start(neg_sink[half, :],
                                   sinks[0:1, s * PAIRS:(s + 1) * PAIRS].to_broadcast([HD, PAIRS])).then_inc(consts_in, 16)
                for g in range(GROUPS):
                    sc.dma_start(pool_map[:, g, :], pool_w_g[:, g, :]).then_inc(consts_in, 16)
            sum_squares_x(0)
            split_w_in(0)
            split_w_in(1)
            xT_high(0)
            for k in range(2, KT):
                if k == 5:
                    sum_squares_x(1)
                split_w_in(k)
            for t in range(NT):
                if t + 1 < NT:
                    xT_high(t + 1)
                if t + 2 < NT:
                    sum_squares_x(t + 2)
                if t == NT - 1:
                    for k in range(5):
                        split_w_out(k)
                if t >= 1:
                    evac_transposed(t - 1)
                copy_in(t)
                if t >= 2:
                    evac_probs(t - 2, (0,))
                copy_u(t)
                if t >= 2:
                    evac_probs(t - 2, (1,))
                if t >= 1:
                    mix_high(t - 1)
                if t >= 2:
                    attention_high(t - 2)
                if t >= 1:
                    exponentials(t - 1)
            for k in range(5, KT):
                split_w_out(k)
            evac_transposed(NT - 1)
            evac_probs(NT - 2)
            mix_high(NT - 1)
            attention_high(NT - 2)
            exponentials(NT - 1)
            sum_squares_x1(0)
            evac_probs(NT - 1)
            sum_squares_x1(1)
            attention_high(NT - 1)
            for t in range(2, NT):
                xT_high(NT + t - 2)
                sum_squares_x1(t)
                if t == 3:
                    split_up(0, 0)
                    split_up(1, 1)
            xT_high(2 * NT - 2)

            def chunk(c, first=False, last=False):
                for n, (f, h) in enumerate(ORDER):
                    N = c * NZ + n
                    if first and n == 2:
                        xT_high(2 * NT - 1)
                    sc.wait_ge(z_done, N + 1)
                    if not (first and n < 2):
                        sc.wait_ge(hid_lo, N - 1)
                    nc.scalar.activation(relu_buf[n % 2], bank[Z_B[n % 2]][:, :], ACT.Relu).then_inc(relu_done, 1)
                    sc.wait_ge(relu_done, N + 1)
                    nc.scalar.activation(relu_buf[n % 2], relu_buf[n % 2], ACT.Square).then_inc(sq_done, 1)
                    sc.wait_ge(sq_done, N + 1)
                    nc.scalar.activation(hid[:, f, HI, h * HALF:(h + 1) * HALF], relu_buf[n % 2],
                                         ACT.Copy).then_inc(hid_hi, 1)
                    if n in (2, 3):
                        split_up(n - 2, c * FC + n)
                    elif n in (4, 5):
                        split_down(c, n - 4)
                if not last:
                    split_up(0, (c + 1) * FC)
                    split_up(1, (c + 1) * FC + 1)

            chunk(0, first=True)
            with sc.Fori(1, NC_FF - 1) as c:
                chunk(c)
            chunk(NC_FF - 1, last=True)

        @block.vector
        def _(dve):
            def xT_low(T):
                t = T % NT
                for i in range(2):
                    dve.wait_ge(xT_hi, 2 * T + i + 1)
                    src = bank[XT_B[T // NT][i]][:, :].rearrange("p (k n) -> p k n", k=4)
                    nc.vector.tensor_tensor(out=act[:, LO, 4 * i:4 * i + 4, tile(t)], in0=src,
                                            in1=act_f[:, HI, 4 * i:4 * i + 4, tile(t)],
                                            op=ALU.subtract).then_inc(xT_lo, 1)

            def normed_x(t):
                dve.wait_ge(rinv_ready, t + 1)
                if t >= 1:
                    dve.wait_ge(xT_done, 2 * t)
                nc.vector.tensor_scalar(out=x_norm, in0=x_slot[t % 2], scalar1=rinv[:, t:t + 1], scalar2=None,
                                        op0=ALU.mult).then_inc(x_norm_ready, 1)

            def normed_x1(t):
                T = NT + t
                dve.wait_ge(rinv_ready, T + 1)
                dve.wait_ge(xT_done, 2 * T)
                dve.wait_ge(tok_added, 2 * t + 2)
                if t == 0:
                    dve.wait_ge(norm2_in, 16)
                nc.vector.scalar_tensor_tensor(out=x_norm, in0=resid[t], scalar=rinv[:, T:T + 1], in1=norm2_row,
                                               op0=ALU.mult, op1=ALU.mult).then_inc(x_norm_ready, 1)

            def split_w_in(k):
                dve.wait_ge(w_in_hi, k + 1)
                nc.vector.scalar_tensor_tensor(out=w_in_s[:, k, LO, :], in0=w_in_stage[k % 6], scalar=g1[:, k:k + 1],
                                               in1=w_in_s[:, k, HI, :].bitcast(F32), op0=ALU.mult,
                                               op1=ALU.subtract).then_inc(w_in_lo, 1)

            def split_w_out(k):
                dve.wait_ge(rows_hi, k + 1)
                nc.vector.tensor_tensor(out=w_out_s[:, k, LO, :], in0=w_out_stage[W_OUT_SLOT[k]],
                                        in1=w_out_s[:, k, HI, :].bitcast(F32), op=ALU.subtract).then_inc(rows_lo, 1)

            def pooled(t):
                dve.wait_ge(win_step, 4 * t + 4)
                sums = [win_a[:, 0, :], win_b[:, 0, :], win_a[:, 2, :], win_b[:, 2, :]]
                if t == 0:
                    for g in range(GROUPS):
                        nc.vector.tensor_tensor(out=sums[g][:, HALO:2 * HALO], in0=sums[g][:, HALO:2 * HALO],
                                                in1=edge[:, g, :], op=ALU.mult).then_inc(pool_step, 1)
                    dve.wait_ge(pool_step, GROUPS)
                for g in range(GROUPS):
                    nc.vector.scalar_tensor_tensor(out=sums[g][:, HALO:UB], in0=sums[g][:, HALO:UB],
                                                   scalar=1.0 / WINDOWS[g], in1=u_T[:, g, HALO:UB],
                                                   op0=ALU.mult, op1=ALU.subtract).then_inc(
                                                       pooled_ready if g == GROUPS - 1 else pool_step, 1)

            def place_values(t):
                dve.wait_ge(kv_copied, t + 1)
                v = qkv[:, Q_W + P:Q_W + KV_W]
                nc.vector.tensor_copy(values[:, t % 4, 1, :], v)
                nc.vector.tensor_copy(values[HD:P, t % 4, 0, :], v[0:HD, :])
                nc.vector.tensor_copy(values[0:HD, (t + 1) % 4, 0, :], v[HD:P, :]).then_inc(values_ready, 1)

            def head_sums(t):
                dve.wait_ge(squares_ready, t + 1)
                nc.vector.reduce_sum(h_ssq, squares.rearrange("p (h d) -> p h d", d=HD), axis=AX.X).then_inc(h_ssq_ready, 1)

            def head_norm(t):
                dve.wait_ge(h_rinv_ready, t + 1)
                qk = qkv[:, 0:Q_W + P].rearrange("p (h d) -> p h d", d=HD)
                scale = h_rinv.rearrange("p (h a) -> p h a", a=1).to_broadcast([P, NH, HD])
                nc.vector.tensor_tensor(out=qk, in0=qk, in1=scale, op=ALU.mult).then_inc(qk_ready, 1)

            def softmax_head(t, cs=(0, 1)):
                for c in cs:
                    n = 2 * t + c
                    dve.wait_ge(scores_done, n + 1)
                    src = bank[SC_B[c]][:, :].rearrange("p (t j) -> p t j", t=PAIRS)
                    lo = CHUNK if n == 0 else 0
                    nc.vector.tensor_tensor(out=scores[c][:, :, lo:], in0=src[:, :, lo:], in1=bias[:, :, lo:],
                                            op=ALU.add).then_inc(biased, 1)
                    dve.wait_ge(biased, n + 1)
                    nc.vector.reduce_max(smax[c], scores[c], axis=AX.X).then_inc(max_ready, 1)
                    dve.wait_ge(max_ready, n + 1)
                    nc.vector.scalar_tensor_tensor(out=neg_max[c], in0=smax[c], scalar=-1.0, in1=neg_sink,
                                                   op0=ALU.mult, op1=ALU.min).then_inc(negmax_ready, 1)
                    dve.wait_ge(negmax_ready, n + 1)
                    nc.vector.tensor_tensor(out=sink_gap[c], in0=neg_max[c], in1=neg_sink,
                                            op=ALU.subtract).then_inc(gap_ready, 1)

            def softmax_tail(t):
                for c in range(2):
                    n = 2 * t + c
                    dve.wait_ge(exp_done, (PAIRS + 1) * (n + 1))
                    nc.vector.tensor_tensor(out=denom[c], in0=row_sum[c], in1=sink_exp[c],
                                            op=ALU.add).then_inc(denom_ready, 1)
                    dve.wait_ge(denom_ready, n + 1)
                    nc.vector.reciprocal(inv_den[c], denom[c]).then_inc(inv_ready, 1)
                    dve.wait_ge(inv_ready, n + 1)
                    for pr in range(PAIRS):
                        nc.vector.tensor_scalar(out=scores[c][:, pr, :], in0=scores[c][:, pr, :],
                                                scalar1=inv_den[c][:, pr:pr + 1], scalar2=None,
                                                op0=ALU.mult).then_inc(probs_ready, 1)

            def mix_low(t):
                dve.wait_ge(mix_hi, GROUPS * (t + 1))
                for g in range(GROUPS):
                    nc.vector.scalar_tensor_tensor(out=act[:, LO, g, tile(t)], in0=bank[MIX_B][:, g * P:(g + 1) * P],
                                                   scalar=pool_sc[:, g:g + 1], in1=act_f[:, HI, g, tile(t)],
                                                   op0=ALU.mult, op1=ALU.subtract).then_inc(mix_lo, 1)

            def attention_low(t):
                for c in range(2):
                    n = 2 * t + c
                    src = bank[OUT_B[c]][:, :].rearrange("p (t s i) -> p s t i", t=PAIRS, s=2)
                    tok = slice(n * CHUNK, (n + 1) * CHUNK)
                    for s in range(2):
                        dve.wait_ge(att_hi, 2 * n + s + 1)
                        half = slice(s * HD, (s + 1) * HD)
                        nc.vector.tensor_tensor(out=act[half, LO, 4:8, tok], in0=src[half, s, :, :],
                                                in1=act_f[half, HI, 4:8, tok], op=ALU.subtract).then_inc(att_lo, 1)

            def add_out(G, t, dh):
                dve.wait_ge(tok_done, G + 1)
                dst = resid[t][:, dh * BANK:(dh + 1) * BANK]
                nc.vector.tensor_tensor(out=dst, in0=bank[TOK_B[(2 * t + dh) % 4 if isinstance(G, int) and G < NTOK
                                                              else (dh * NT + t) % 4]][:, :],
                                        in1=dst, op=ALU.add).then_inc(tok_added, 1)

            def add_x1(t):
                dve.wait_ge(resid_in[t], 16)
                add_out(2 * t, t, 0)
                add_out(2 * t + 1, t, 1)

            def split_up(slot, U):
                dve.wait_ge(up_hi, U + 1)
                nc.vector.tensor_tensor(out=up_s[slot][:, LO, :, :], in0=up_stage[slot],
                                        in1=up_s[slot][:, HI, :, :].bitcast(F32), op=ALU.subtract).then_inc(up_lo, 1)

            def split_down(c, dh):
                dve.wait_ge(rows_hi, c * 2 + KT + dh + 1)
                nc.vector.tensor_tensor(out=down_s[dh][:, LO, :, :], in0=down_stage[dh],
                                        in1=down_s[dh][:, HI, :, :].bitcast(F32), op=ALU.subtract).then_inc(rows_lo, 1)

            normed_x(0)
            split_w_in(0)
            split_w_in(1)
            xT_low(0)
            for k in range(2, KT):
                if k == 5:
                    normed_x(1)
                split_w_in(k)
            dve.wait_ge(w_in_lo, KT)
            nc.vector.memset(keys_T[:, 0:CHUNK], 0.0).then_inc(zeroed, 1)
            nc.vector.memset(q_diag, 0.0).then_inc(zeroed, 1)
            nc.vector.memset(u_T[:, :, 0:HALO], 0.0).then_inc(zeroed, 1)
            nc.vector.memset(values[0:HD, 0, 0, :], 0.0).then_inc(zeroed, 1)
            dve.wait_ge(zeroed, 4)
            nc.vector.memset(scores[0][:, :, 0:CHUNK], MASK).then_inc(pads_ready, 1)
            dve.wait_ge(pads_ready, 1)
            dve.wait_ge(setup_pool, 6)
            dve.wait_ge(consts_in, 16 * N_CONST)
            steps = [0]

            def step(ins):
                steps[0] += 1
                ins.then_inc(setup_dve, 1)
                dve.wait_ge(setup_dve, steps[0])

            step(nc.vector.scalar_tensor_tensor(out=dist, in0=dist, scalar=-1.0, in1=dist, op0=ALU.mult, op1=ALU.max))
            for pr in range(PAIRS):
                for s in range(2):
                    half = slice(s * HD, (s + 1) * HD)
                    slope = 2.0 ** (-8.0 * (pr + s * PAIRS + 1) / NQ)
                    step(nc.vector.tensor_scalar(out=bias[half, pr, :], in0=dist[half, :], scalar1=-slope,
                                                 scalar2=None, op0=ALU.mult))
            for g, w in enumerate(WINDOWS):
                step(nc.vector.tensor_scalar(out=edge[:, g, :], in0=edge[:, g, :], scalar1=float(w), scalar2=None,
                                             op0=ALU.min))
            step(nc.vector.reciprocal(edge, edge))
            for g, w in enumerate(WINDOWS):
                step(nc.vector.tensor_scalar(out=edge[:, g, :], in0=edge[:, g, :], scalar1=float(w), scalar2=None,
                                             op0=ALU.mult))
            step(nc.vector.tensor_scalar(out=q_gain, in0=q_gain, scalar1=HD ** -0.5, scalar2=None, op0=ALU.mult))
            nc.vector.tensor_scalar(out=neg_sink, in0=neg_sink, scalar1=-1.0, scalar2=None,
                                    op0=ALU.mult).then_inc(setup_done, 1)
            dve.wait_ge(setup_done, 1)

            for t in range(NT):
                if t + 1 < NT:
                    xT_low(t + 1)
                if t + 2 < NT:
                    normed_x(t + 2)
                if t == NT - 1:
                    for k in range(5):
                        split_w_out(k)
                if t >= 1:
                    pooled(t - 1)
                place_values(t)
                head_sums(t)
                if t >= 1:
                    softmax_head(t - 1, (0,))
                    mix_low(t - 1)
                    softmax_head(t - 1, (1,))
                if t >= 2:
                    attention_low(t - 2)
                head_norm(t)
                if t >= 1:
                    softmax_tail(t - 1)
            for k in range(5, KT):
                split_w_out(k)
            pooled(NT - 1)
            softmax_head(NT - 1)
            mix_low(NT - 1)
            attention_low(NT - 2)
            softmax_tail(NT - 1)
            add_x1(0)
            normed_x1(0)
            add_x1(1)
            attention_low(NT - 1)
            for t in range(2, NT):
                xT_low(NT + t - 2)
                normed_x1(t - 1)
                add_x1(t)
                if t == 3:
                    split_up(0, 0)
                    split_up(1, 1)
            xT_low(2 * NT - 2)
            normed_x1(NT - 1)

            def chunk(c, first=False, last=False):
                for n, (f, h) in enumerate(ORDER):
                    if first and n == 2:
                        xT_low(2 * NT - 1)
                    dve.wait_ge(hid_hi, c * NZ + n + 1)
                    half = slice(h * HALF, (h + 1) * HALF)
                    nc.vector.tensor_tensor(out=hid[:, f, LO, half], in0=relu_buf[n % 2],
                                            in1=hid[:, f, HI, half].bitcast(F32), op=ALU.subtract).then_inc(hid_lo, 1)
                    if n in (2, 3):
                        split_up(n - 2, c * FC + n)
                    elif n in (4, 5):
                        split_down(c, n - 4)
                if not last:
                    split_up(0, (c + 1) * FC)
                    split_up(1, (c + 1) * FC + 1)
                for dh in range(2):
                    for t in range(NT):
                        G = (c + 1) * NTOK + dh * NT + t
                        dve.wait_ge(tok_added, G - NTOK + 1)
                        add_out(G, t, dh)

            chunk(0, first=True)
            with dve.Fori(1, NC_FF - 1) as c:
                chunk(c)
            chunk(NC_FF - 1, last=True)

        @block.tensor
        def _(pe):
            def passes(out_ap, lhs, rhs, first, last):
                nc.tensor.matmul(out_ap, lhs[HI], rhs[HI], start=first, stop=False)
                nc.tensor.matmul(out_ap, lhs[HI], rhs[LO], start=False, stop=False)
                return nc.tensor.matmul(out_ap, lhs[LO], rhs[HI], start=False, stop=last)

            def transpose_x(T):
                stage = T // NT
                pe.wait_ge(x_norm_ready, T + 1)
                if T == 0:
                    pe.wait_ge(setup_pool, 6)
                if stage == 0 and T >= 3:
                    pe.wait_ge(mix_lo, GROUPS * (T - 2))
                    if T >= 4:
                        pe.wait_ge(att_lo, 4 * (T - 3))
                if stage == 0 and T == 1:
                    pe.wait_ge(xT_lo, 2)
                if stage == 1 and T > NT:
                    pe.wait_ge(xT_lo, 2 * T)
                for i in range(2):
                    for k in range(4):
                        last = nc.tensor.transpose(bank[XT_B[stage][i]][:, k * P:(k + 1) * P],
                                                   x_norm[:, (4 * i + k) * P:(4 * i + k + 1) * P], ident)
                    last.then_inc(xT_done, 1)

            def project_in(t, ks):
                lhs = lambda k: [act[:, part, k, tile(t)] for part in (HI, LO)]
                rhs = lambda k, a, n: [w_in_s[:, k, part, a:a + n] for part in (HI, LO)]
                for k in ks:
                    if k == 0:
                        pe.wait_ge(xT_lo, 2 * (t + 1))
                        if t >= 1:
                            pe.wait_ge(kv_copied, t)
                            pe.wait_ge(q_copied, t)
                            pe.wait_ge(u_copied, t)
                    if t == 0:
                        pe.wait_ge(w_in_lo, k + 1)
                    first, stop = k == 0, k == KT - 1
                    passes(bank[KV_B][:, 0:KV_W], lhs(k), rhs(k, POOL_W + Q_W, KV_W), first, stop)
                    passes(bank[Q_B][:, :], lhs(k), rhs(k, POOL_W, Q_W), first, stop)
                    last = passes(bank[U_B][:, :], lhs(k), rhs(k, 0, POOL_W), first, stop)
                    last.then_inc(in_done, 1)

            def project_out(t, ks):
                for k in ks:
                    if k == 0:
                        for dh in range(2):
                            if 2 * t + dh >= 4:
                                pe.wait_ge(tok_added, 2 * t + dh - 3)
                        if t == 0:
                            pe.wait_ge(kv_copied, NT)
                            pe.wait_ge(q_copied, NT)
                        if t == 1:
                            pe.wait_ge(u_copied, NT)
                            pe.wait_ge(mix_lo, GROUPS * NT)
                        if t == NT - 1:
                            pe.wait_ge(mix_lo, GROUPS * NT)
                    if k == KT // 2:
                        pe.wait_ge(att_lo, 4 * (t + 1))
                    if t == 0:
                        pe.wait_ge(rows_lo, k + 1)
                    for dh in range(2):
                        cols = slice(dh * BANK, (dh + 1) * BANK)
                        last = passes(bank[TOK_B[(2 * t + dh) % 4]][:, :],
                                      [act[:, part, k, tile(t)] for part in (HI, LO)],
                                      [w_out_s[:, k, part, cols] for part in (HI, LO)], k == 0, k == KT - 1)
                        if k == KT - 1:
                            last.then_inc(tok_done, 1)

            def transpose_in(t):
                pe.wait_ge(u_copied, t + 1)
                if t + 2 < NT:
                    pe.wait_ge(xT_lo, 2 * (t + 3))
                else:
                    pe.wait_ge(mix_lo, GROUPS * t)
                    pe.wait_ge(att_lo, 4 * (t - 1))
                for g in range(GROUPS):
                    last = nc.tensor.transpose(bank[UT_B][:, g * P:(g + 1) * P], u_tok[:, g * P:(g + 1) * P], ident)
                last.then_inc(uT_done, 1)
                pe.wait_ge(qk_ready, t + 1)
                for pr in range(PAIRS):
                    last = nc.tensor.transpose(bank[QT_B][:, pr * P:(pr + 1) * P], qkv[:, pr * P:(pr + 1) * P], ident)
                last.then_inc(qT_done, 1)
                if t >= 2:
                    pe.wait_ge(att_lo, 4 * (t - 1))
                nc.tensor.transpose(bank[KT_B][:, 0:P], qkv[:, Q_W:Q_W + P], ident).then_inc(kT_done, 1)

            def transpose_probs(t):
                for c in range(2):
                    pe.wait_ge(probs_ready, PAIRS * (2 * t + c + 1))
                    for pr in range(PAIRS):
                        last = nc.tensor.transpose(bank[SC_B[c]][:, pr * P:(pr + 1) * P], scores[c][:, pr, :], ident)
                    last.then_inc(pT_done, 1)

            def mix(t):
                pe.wait_ge(pooled_ready, t + 1)
                pe.wait_ge(u_T_ready, t + 1)
                windows = [win_a[:, 0, :], win_b[:, 0, :], win_a[:, 2, :], win_b[:, 2, :]]
                for g in range(GROUPS):
                    last = nc.tensor.matmul(bank[MIX_B][:, g * P:(g + 1) * P], pool_map[:, g, :],
                                            windows[g][:, HALO:UB], start=True, stop=True)
                last.then_inc(mix_done, 1)

            def score(t):
                pe.wait_ge(q_diag_ready, 2 * (t + 1))
                pe.wait_ge(keys_ready, t + 1)
                for c in range(2):
                    n = 2 * t + c
                    if t >= 1:
                        pe.wait_ge(pT_copied, n - 1)
                    for pr in range(PAIRS):
                        last = nc.tensor.matmul(bank[SC_B[c]][:, pr * P:(pr + 1) * P], q_diag[:, c, pr, :],
                                                keys_T[:, n * CHUNK:(n + 2) * CHUNK], start=True, stop=True)
                    last.then_inc(scores_done, 1)

            def attend(t):
                pe.wait_ge(values_ready, t + 1)
                if t + 1 < NT:
                    pe.wait_ge(q_diag_ready, 2 * (t + 2))
                    pe.wait_ge(keys_ready, t + 2)
                for c in range(2):
                    n = 2 * t + c
                    pe.wait_ge(pT_copied, n + 1)
                    nc.tensor.matmul(bank[OUT_B[c]][:, :], values[:, t % 4, c, :], probs_T[c],
                                     start=True, stop=True).then_inc(pv_done, 1)

            transpose_x(0)
            for t in range(NT):
                a, b = (6, 6) if t == 0 else (2, 5)
                project_in(t, range(0, a))
                if t + 1 < NT:
                    transpose_x(t + 1)
                project_in(t, range(a, b))
                if t >= 1:
                    transpose_in(t - 1)
                project_in(t, range(b, KT))
                if t >= 2:
                    transpose_probs(t - 2)
                if t >= 1:
                    mix(t - 1)
                    score(t - 1)
                if t >= 2:
                    attend(t - 2)
            project_out(0, range(0, 3))
            transpose_in(NT - 1)
            project_out(0, range(3, 6))
            transpose_probs(NT - 2)
            mix(NT - 1)
            score(NT - 1)
            attend(NT - 2)
            project_out(0, range(6, KT))
            project_out(1, range(KT))
            transpose_probs(NT - 1)
            project_out(2, range(0, 3))
            attend(NT - 1)
            transpose_x(NT)
            project_out(2, range(3, KT))
            for t in range(3, NT):
                transpose_x(NT + t - 2)
                project_out(t, range(KT))
            transpose_x(2 * NT - 2)

            def hidden(c, n, first):
                f, h = ORDER[n]
                slot = f % 2
                if h == 0:
                    pe.wait_ge(up_lo, c * FC + f + 1)
                if first and n == 0:
                    pe.wait_ge(att_lo, 4 * NT)
                if first and n < 4:
                    pe.wait_ge(xT_lo, 2 * (NT + NT // 2 * (h + 1)))
                if not (first and n < 2):
                    pe.wait_ge(relu_done, c * NZ + n - 1)
                half = slice(h * HALF, (h + 1) * HALF)
                for k in range(KT):
                    last = passes(bank[Z_B[n % 2]][:, :], [up_s[slot][:, part, k, :] for part in (HI, LO)],
                                  [act[:, part, k, half] for part in (HI, LO)], k == 0, k == KT - 1)
                last.then_inc(z_done, 1)

            def down(c):
                for dh in range(2):
                    pe.wait_ge(rows_lo, c * 2 + KT + dh + 1)
                    for t in range(NT):
                        g = dh * NT + t
                        pe.wait_ge(tok_added, (c + 1) * NTOK + g - 3)
                        if t % (NT // 2) == 0 and dh == 0:
                            pe.wait_ge(hid_lo, c * NZ + (NZ - 2 if t == 0 else NZ))
                        for f in range(FC):
                            last = passes(bank[TOK_B[g % 4]][:, :], [hid[:, f, part, tile(t)] for part in (HI, LO)],
                                          [down_s[dh][:, part, f, :] for part in (HI, LO)], f == 0, f == FC - 1)
                        last.then_inc(tok_done, 1)

            hidden(0, 0, True)
            hidden(0, 1, True)
            transpose_x(2 * NT - 1)
            for n in range(2, NZ):
                hidden(0, n, True)
            down(0)
            with pe.Fori(1, NC_FF) as c:
                for n in range(NZ):
                    hidden(c, n, False)
                down(c)


_INS = ["x", "norm1_g", "w_in", "pool_w", "pool_scale", "q_norm_g", "k_norm_g", "sinks",
        "w_out", "norm2_g", "w_up", "w_down"]


def kernel(**inputs):
    import numpy as np
    import concourse.bacc as bacc
    from concourse.bass_utils import run_bass_kernel_spmd

    nc = bacc.Bacc("TRN2", target_bir_lowering=False, num_devices=1)
    arrays, args = {}, []
    for name in _INS:
        a = np.ascontiguousarray(inputs[name])
        arrays[f"in_{name}"] = a
        args.append(nc.dram_tensor(f"in_{name}", a.shape, mybir.dt.from_np(a.dtype), kind="ExternalInput").ap())
    shape = arrays["in_x"].shape
    args.append(nc.dram_tensor("out_x", shape, F32, kind="ExternalOutput").ap())
    hybrid_trunk(nc, *args)
    result = run_bass_kernel_spmd(nc, [arrays], core_ids=[0])
    return result.results[0]["out_x"]
```

```python
import concourse.bass as bass
from concourse import mybir
from contextlib import ExitStack

F32 = mybir.dt.float32
F32R = mybir.dt.float32r
BF16 = mybir.dt.bfloat16
ALU = mybir.AluOpType
ACT = mybir.ActivationFunctionType
AX = mybir.AxisListType

P = 128
BANK = 512
HI, LO = 0, 1


def hybrid_trunk(nc, x, norm1_g, w_in, pool_w, pool_scale, q_norm_g, k_norm_g, sinks,
                 w_out, norm2_g, w_up, w_down, out):
    SEQ, D = x.shape[1], x.shape[2]
    IN_W = w_in.shape[2]
    GROUPS = pool_w.shape[1]
    POOL_W = pool_scale.shape[1]
    HD = q_norm_g.shape[1]
    NQ = sinks.shape[1]
    D_FF = w_up.shape[2]
    CHUNK = HD
    Q_W = NQ * HD
    KT = D // P
    NT = SEQ // P
    NCH = 2 * NT
    PAIRS = NQ // 2
    WINDOWS = [2 << g for g in range(GROUPS)]
    HALO = WINDOWS[-1]
    EPS = 1e-6
    MASK = -1e30
    FC = 4
    CH_FF = FC * P
    NC_FF = D_FF // CH_FF
    assert KT == 8 and NT == 8 and PAIRS == 4 and IN_W == POOL_W + Q_W + 2 * P and D == 2 * BANK

    x_t = x[0].rearrange("(t p) d -> t p d", p=P)
    out_t = out[0].rearrange("(t p) d -> t p d", p=P)
    w_in_k = w_in[0].rearrange("(k p) e -> k p e", p=P)
    w_out_k = w_out[0].rearrange("(k p) n -> k p n", p=P)
    w_up_k = w_up[0].rearrange("(k p) f -> p k f", p=P)
    w_down_c = w_down[0].rearrange("(c f p) n -> c p f n", p=P, f=FC)
    pool_w_g = pool_w[0].rearrange("g c d -> c g d")

    with ExitStack() as ctx:
        def sem(name):
            return ctx.enter_context(nc.semaphore(name))

        act = ctx.enter_context(nc.sbuf_tensor("act", [P, 2, KT, SEQ], F32R))
        act_f = act[:, :, :, :].bitcast(F32)
        WGT = 2 * KT * IN_W
        wgt = ctx.enter_context(nc.sbuf_tensor("wgt", [P, WGT], F32R))
        w_in_s = wgt[:, :].rearrange("p (k h e) -> p k h e", k=KT, h=2)
        w_out_s = wgt[:, 0:2 * KT * D].rearrange("p (k h n) -> p k h n", k=KT, h=2)
        hid = wgt[:, 0:2 * FC * SEQ].rearrange("p (f h s) -> p f h s", f=FC, h=2)
        DN0 = 2 * FC * SEQ
        DNW = 2 * FC * BANK
        down_s = [wgt[:, DN0 + i * DNW:DN0 + (i + 1) * DNW].rearrange("p (h f n) -> p h f n", h=2, f=FC)
                  for i in range(2)]
        UP0 = DN0 + 2 * DNW
        UPW = 2 * KT * P
        up_s = [wgt[:, UP0 + i * UPW:UP0 + (i + 1) * UPW].rearrange("p (h k n) -> p h k n", h=2, k=KT)
                for i in range(2)]
        assert UP0 + 2 * UPW <= WGT

        FREE = 16336
        mem = ctx.enter_context(nc.sbuf_tensor("mem", [P, FREE], F32))
        at = [0]

        def take(words):
            a = at[0]
            at[0] += words
            assert at[0] <= FREE
            return a

        def view(a, words):
            return mem[:, a:a + words]

        KV_W = 2 * P
        UB = HALO + P
        a_x = take(2 * D)
        a_A = take(2 * D)
        a_B = take(4 * D)
        a_C = take(3 * D)
        a_ws = take(2 * D)
        a_xn = take(D)
        a_bp = take(D)
        a_junk = take(D // 2)
        x_slot = [view(a_x + i * D, D) for i in range(2)]
        u_tok = view(a_A, POOL_W)
        qkv = view(a_A + POOL_W, Q_W + KV_W)
        squares = view(a_A + POOL_W + Q_W + KV_W, Q_W + P)
        b = a_B
        keys_T = view(b, CHUNK + SEQ); b += CHUNK + SEQ
        q_diag = view(b, 2 * PAIRS * P).rearrange("p (c t n) -> p c t n", c=2, t=PAIRS); b += 2 * PAIRS * P
        u_T = view(b, GROUPS * UB).rearrange("p (g s) -> p g s", g=GROUPS); b += GROUPS * UB
        win_a = view(b, GROUPS * UB).rearrange("p (g s) -> p g s", g=GROUPS); b += GROUPS * UB
        win_b = view(b, 3 * UB).rearrange("p (g s) -> p g s", g=3); b += 3 * UB
        assert b <= a_B + 4 * D
        scores = [view(a_C + i * BANK, BANK).rearrange("p (t j) -> p t j", t=PAIRS) for i in range(2)]
        probs_T = [view(a_C + D + i * BANK, BANK) for i in range(2)]
        values = view(a_C + 2 * D, 8 * P).rearrange("p (r c n) -> p r c n", r=4, c=2)
        x_norm = view(a_xn, D)
        gain_rows = view(a_xn, P)[0:KT + GROUPS, :]
        bias = view(a_bp, BANK).rearrange("p (t j) -> p t j", t=PAIRS)
        pool_map = view(a_bp + BANK, BANK).rearrange("p (g n) -> p g n", g=GROUPS)
        junk = view(a_junk, D // 2).bitcast(BF16)
        w_in_stage = ([view(a_C + i * IN_W, IN_W) for i in range(2)] + [view(a_A, IN_W)]
                      + [view(a_B + i * IN_W, IN_W) for i in range(3)])
        w_out_stage = [view(a, D) for a in (a_ws, a_ws + D, a_x, a_x + D, a_xn)]
        W_OUT_SLOT = [0, 1, 2, 3, 4, 0, 1, 4]
        dist = view(a_ws, P)
        resid = ([view(a_x + i * D, D) for i in range(2)] + [view(a_A + i * D, D) for i in range(2)]
                 + [view(a_B + i * D, D) for i in range(4)])
        norm2_row = view(a_bp, D)
        up_stage = [view(a_C + i * D, D).rearrange("p (k n) -> p k n", k=KT) for i in range(2)]
        relu_buf = [view(a_C + 2 * D + i * BANK, BANK) for i in range(2)]
        down_stage = [view(a_ws, 2 * D).rearrange("p (f n) -> p f n", f=FC),
                      view(a_xn, 2 * D).rearrange("p (f n) -> p f n", f=FC)]
        ident = view(take(P), P)
        small = lambda n: view(take(n), n)
        gains = small(KT + GROUPS)
        g1, pool_sc = gains[:, 0:KT], gains[:, KT:KT + GROUPS]
        q_gain, k_gain = small(1), small(1)
        neg_sink = small(PAIRS)
        NH = NQ + 2
        minus_half = small(NH)
        edge = small(GROUPS * HALO).rearrange("p (g j) -> p g j", g=GROUPS)
        ssq, var, rinv = small(2 * NT), small(2 * NT), small(2 * NT)
        h_ssq, h_var, h_rinv = small(NH), small(NH), small(NH)
        pair = lambda: [small(PAIRS) for _ in range(2)]
        smax, neg_max, sink_gap, sink_exp, row_sum, denom, inv_den = (pair() for _ in range(7))

        bank = [ctx.enter_context(nc.psum_tensor(f"bank{i}", [P, BANK], F32)) for i in range(8)]
        KV_B, Q_B, U_B = 2, 3, 4
        XT_B = [[0, 1], [5, 6]]
        UT_B, QT_B, KT_B = 0, 1, 7
        GAIN_B = 7
        MIX_B, SC_B, OUT_B = 0, [5, 6], [7, 1]
        TOK_B = [2, 3, 4, 0]
        Z_B = [1, 7]

        gain_rows_in, consts_in = sem("gain_rows_in"), sem("consts_in")
        x_in = [sem(f"x_in{i}") for i in range(2)]
        resid_in = [sem(f"resid_in{i}") for i in range(NT)]
        norm2_in = sem("norm2_in")
        w_in_in = [sem(f"w_in_in{i}") for i in range(6)]
        w_out_in = [sem(f"w_out_in{i}") for i in range(5)]
        up_in = [sem(f"up_in{i}") for i in range(2)]
        down_in = [sem(f"down_in{i}") for i in range(2)]
        stored = sem("stored")
        zeroed, setup_pool, setup_dve, setup_done = sem("zeroed"), sem("setup_pool"), sem("setup_dve"), sem("setup_done")
        pads_ready = sem("pads_ready")
        gains_done, gains_ready = sem("gains_done"), sem("gains_ready")
        sumsq_ready, var_ready, rinv_ready, x_norm_ready = sem("sumsq_ready"), sem("var_ready"), sem("rinv_ready"), sem("x_norm_ready")
        xT_done, xT_hi, xT_lo = sem("xT_done"), sem("xT_hi"), sem("xT_lo")
        w_in_hi, w_in_lo = sem("w_in_hi"), sem("w_in_lo")
        w_in_first_hi, w_in_first_lo = sem("w_in_first_hi"), sem("w_in_first_lo")
        rows_hi, rows_lo = sem("rows_hi"), sem("rows_lo")
        up_hi, up_lo = sem("up_hi"), sem("up_lo")
        in_done = sem("in_done")
        kv_done, q_done = sem("kv_done"), sem("q_done")
        kv_copied, q_copied, u_copied = sem("kv_copied"), sem("q_copied"), sem("u_copied")
        squares_ready, h_ssq_ready, h_var_ready, h_rinv_ready, qk_ready = (sem(n) for n in (
            "squares_ready", "h_ssq_ready", "h_var_ready", "h_rinv_ready", "qk_ready"))
        values_ready = sem("values_ready")
        uT_done, qT_done, kT_done = sem("uT_done"), sem("qT_done"), sem("kT_done")
        halo_ready, u_T_ready, q_diag_ready, keys_ready = sem("halo_ready"), sem("u_T_ready"), sem("q_diag_ready"), sem("keys_ready")
        win_step, pool_step, pooled_ready = sem("win_step"), sem("pool_step"), sem("pooled_ready")
        mix_done, mix_hi, mix_lo = sem("mix_done"), sem("mix_hi"), sem("mix_lo")
        scores_done, biased, max_ready, negmax_ready, gap_ready = (sem(n) for n in (
            "scores_done", "biased", "max_ready", "negmax_ready", "gap_ready"))
        exp_done, denom_ready, inv_ready, probs_ready = (sem(n) for n in (
            "exp_done", "denom_ready", "inv_ready", "probs_ready"))
        pT_done, pT_copied, pv_done, att_hi, att_lo = (sem(n) for n in (
            "pT_done", "pT_copied", "pv_done", "att_hi", "att_lo"))
        tok_done, tok_added = sem("tok_done"), sem("tok_added")
        z_done, relu_done, sq_done, hid_hi, hid_lo = (sem(n) for n in (
            "z_done", "relu_done", "sq_done", "hid_hi", "hid_lo"))

        N_CONST = 6 + GROUPS
        HALF = SEQ // 2
        ORDER = [(2 * p + i, h) for p in range(FC // 2) for h in range(2) for i in range(2)]
        NZ = len(ORDER)
        NTOK = 2 * NT

        def tile(t):
            return slice(t * P, (t + 1) * P)

        block = ctx.enter_context(nc.Block())

        @block.sync
        def _(sp):
            def load_x(t):
                if t >= 2:
                    sp.wait_ge(xT_done, 2 * (t - 1))
                    sp.wait_ge(sumsq_ready, t - 1)
                sp.dma_start(x_slot[t % 2], x_t[t]).then_inc(x_in[t % 2], 16)

            def load_w_in(k):
                if k >= 6:
                    sp.wait_ge(w_in_lo, k - 5)
                sp.dma_start(w_in_stage[k % 6], w_in_k[k]).then_inc(w_in_in[k % 6], 16)

            def load_w_out(k):
                slot = W_OUT_SLOT[k]
                if slot in W_OUT_SLOT[:k]:
                    sp.wait_ge(rows_lo, W_OUT_SLOT.index(slot) + 1)
                dst, done = w_out_stage[slot], w_out_in[slot]
                if k < KT // 2:
                    sp.dma_start(dst, w_out_k[k]).then_inc(done, 16)
                else:
                    for s in range(2):
                        r = POOL_W + (s * PAIRS + k - KT // 2) * HD
                        sp.dma_start(dst[s * HD:(s + 1) * HD, :], w_out[0, r:r + HD, :]).then_inc(done, 16)

            def load_up(slot, c, f):
                sp.dma_start(up_stage[slot], w_up_k[:, :, bass.ds(c * CH_FF + f * P, P)]).then_inc(up_in[slot], 16)

            def load_down(c, dh):
                sp.dma_start(down_stage[dh], w_down_c[c, :, :, dh * BANK:(dh + 1) * BANK]).then_inc(down_in[dh], 16)

            load_x(0)
            for k in range(KT):
                load_w_in(k)
            load_x(1)
            with nc.allow_non_contiguous_dma(reason="small per-partition gains"):
                for s in range(2):
                    half = slice(s * HD, (s + 1) * HD)
                    sp.dma_start(q_gain[half, :], q_norm_g[0].rearrange("(p a) -> p a", a=1)).then_inc(consts_in, 16)
                    sp.dma_start(k_gain[half, :], k_norm_g[0].rearrange("(p a) -> p a", a=1)).then_inc(consts_in, 16)
                    sp.dma_start(neg_sink[half, :],
                                   sinks[0:1, s * PAIRS:(s + 1) * PAIRS].to_broadcast([HD, PAIRS])).then_inc(consts_in, 16)
                for g in range(GROUPS):
                    sp.dma_start(pool_map[:, g, :], pool_w_g[:, g, :]).then_inc(consts_in, 16)
            for t in range(2, NT):
                load_x(t)
            sp.wait_ge(setup_done, 1)
            load_w_out(0)
            load_w_out(1)
            sp.wait_ge(xT_done, 2 * (NT - 1))
            sp.wait_ge(sumsq_ready, NT - 1)
            load_w_out(2)
            sp.wait_ge(xT_done, 2 * NT)
            sp.wait_ge(sumsq_ready, NT)
            load_w_out(3)
            sp.wait_ge(gains_done, 1)
            load_w_out(4)
            for k in range(5, KT):
                load_w_out(k)
            sp.wait_ge(rows_lo, 4)
            for t in range(2):
                sp.dma_start(resid[t], x_t[t]).then_inc(resid_in[t], 16)
            sp.wait_ge(uT_done, NT)
            sp.wait_ge(kT_done, NT)
            sp.wait_ge(values_ready, NT)
            for t in range(2, 4):
                sp.dma_start(resid[t], x_t[t]).then_inc(resid_in[t], 16)
            sp.wait_ge(mix_done, NT)
            sp.wait_ge(scores_done, NCH)
            sp.wait_ge(biased, NCH)
            sp.dma_start(norm2_row, norm2_g.to_broadcast([P, D])).then_inc(norm2_in, 16)
            for t in range(4, NT):
                sp.dma_start(resid[t], x_t[t]).then_inc(resid_in[t], 16)
            sp.wait_ge(pv_done, NCH)
            load_up(0, 0, 0)
            load_up(1, 0, 1)

            def chunk(c, first=False, last=False):
                U = c * FC
                sp.wait_ge(up_lo, U + 1)
                load_up(0, c, 2)
                sp.wait_ge(up_lo, U + 2)
                load_up(1, c, 3)
                if first:
                    sp.wait_ge(xT_done, 4 * NT)
                sp.wait_ge(rows_lo, c * 2 + KT - 1)
                load_down(c, 0)
                sp.wait_ge(rows_lo, c * 2 + KT)
                load_down(c, 1)
                if not last:
                    sp.wait_ge(up_lo, U + 3)
                    load_up(0, c + 1, 0)
                    sp.wait_ge(up_lo, U + 4)
                    load_up(1, c + 1, 1)

            chunk(0, first=True)
            with sp.Fori(1, NC_FF - 1) as c:
                chunk(c)
            chunk(NC_FF - 1, last=True)
            for g in range(NTOK):
                dh, t = divmod(g, NT)
                sp.wait_ge(tok_added, NTOK * NC_FF + g + 1)
                sp.dma_start(out_t[t][:, dh * BANK:(dh + 1) * BANK],
                             resid[t][:, dh * BANK:(dh + 1) * BANK]).then_inc(stored, 16)
            sp.wait_ge(stored, 16 * NTOK)

        @block.gpsimd
        def _(pool):
            nc.gpsimd.memset(ident, 0.0).then_inc(setup_pool, 1)
            nc.gpsimd.memset(minus_half, -0.5).then_inc(setup_pool, 1)
            pool.wait_ge(setup_pool, 2)
            nc.gpsimd.affine_select(out=ident, in_=ident, compare_op=ALU.not_equal, fill=1.0, base=0,
                                    pattern=[[-1, P]], channel_multiplier=1).then_inc(setup_pool, 1)
            for s in range(2):
                pool.wait_ge(setup_pool, 3 + s)
                nc.gpsimd.iota(dist[s * HD:(s + 1) * HD, :], [[-1, P]], base=CHUNK, channel_multiplier=1,
                               allow_small_or_imprecise_dtypes=True).then_inc(setup_pool, 1)
            pool.wait_ge(setup_pool, 5)
            nc.gpsimd.iota(edge, [[0, GROUPS], [1, HALO]], base=1, channel_multiplier=0,
                           allow_small_or_imprecise_dtypes=True).then_inc(setup_pool, 1)
            pool.wait_ge(setup_pool, 6)

            def inverse_rms(T):
                pool.wait_ge(sumsq_ready, T + 1)
                nc.gpsimd.tensor_scalar(out=var[:, T:T + 1], in0=ssq[:, T:T + 1], scalar1=1.0 / D, scalar2=EPS,
                                        op0=ALU.mult, op1=ALU.add).then_inc(var_ready, 1)
                pool.wait_ge(var_ready, T + 1)
                nc.gpsimd.tensor_tensor(out=rinv[:, T:T + 1], in0=var[:, T:T + 1], in1=minus_half[:, 0:1],
                                        op=ALU.pow).then_inc(rinv_ready, 1)

            def window_sums(t):
                pool.wait_ge(u_T_ready, t + 1)
                if t == 0:
                    pool.wait_ge(pads_ready, 1)
                if t >= 1:
                    pool.wait_ge(mix_done, t)
                sums = [(win_a, 0, u_T, 0, 0, 1), (win_b, 0, win_a, 1, 1, 2),
                        (win_a, 2, win_b, 1, 2, 4), (win_b, 2, win_a, 3, 3, 8)]
                for n, (dst, d0, src, s0, g0, shift) in enumerate(sums):
                    cnt, lo = GROUPS - g0, 2 * shift - 1
                    if n:
                        pool.wait_ge(win_step, 4 * t + n)
                    nc.gpsimd.tensor_tensor(out=dst[:, d0:d0 + cnt, lo:UB], in0=src[:, s0:s0 + cnt, lo:UB],
                                            in1=src[:, s0:s0 + cnt, lo - shift:UB - shift],
                                            op=ALU.add).then_inc(win_step, 1)

            def head_squares(t):
                pool.wait_ge(q_copied, t + 1)
                pool.wait_ge(kv_copied, t + 1)
                qk = qkv[:, 0:Q_W + P]
                nc.gpsimd.tensor_tensor(out=squares, in0=qk, in1=qk, op=ALU.mult).then_inc(squares_ready, 1)

            def head_inverse_rms(t):
                pool.wait_ge(h_ssq_ready, t + 1)
                nc.gpsimd.tensor_scalar(out=h_var, in0=h_ssq, scalar1=1.0 / HD, scalar2=EPS,
                                        op0=ALU.mult, op1=ALU.add).then_inc(h_var_ready, 1)
                pool.wait_ge(h_var_ready, t + 1)
                nc.gpsimd.tensor_tensor(out=h_rinv, in0=h_var, in1=minus_half, op=ALU.pow).then_inc(h_rinv_ready, 1)

            inverse_rms(0)
            for t in range(NT + 2):
                if 1 <= t < NT - 1:
                    inverse_rms(t + 1)
                if 0 <= t - 1 < NT:
                    window_sums(t - 1)
                if t < NT:
                    head_squares(t)
                    head_inverse_rms(t)
                    if t == 0:
                        inverse_rms(1)
                else:
                    inverse_rms(t)
            for T in range(NT + 2, 2 * NT):
                inverse_rms(T)

        @block.scalar
        def _(sc):
            def sum_squares(T, src):
                if T >= 1:
                    sc.wait_ge(sumsq_ready, T)
                nc.scalar.activation(junk, src, ACT.Square, accum_out=ssq[:, T:T + 1]).then_inc(sumsq_ready, 1)

            def sum_squares_x(t):
                sc.wait_ge(x_in[t % 2], 16 * (t // 2 + 1))
                sum_squares(t, x_slot[t % 2])

            def sum_squares_x1(t):
                sc.wait_ge(tok_added, 2 * t + 2)
                sum_squares(NT + t, resid[t])

            def xT_high(T):
                t = T % NT
                for i in range(2):
                    sc.wait_ge(xT_done, 2 * T + i + 1)
                    src = bank[XT_B[T // NT][i]][:, :].rearrange("p (k n) -> p k n", k=4)
                    nc.scalar.activation(act[:, HI, 4 * i:4 * i + 4, tile(t)], src, ACT.Copy).then_inc(xT_hi, 1)

            def split_first_w_in():
                sc.wait_ge(gains_ready, 1)
                sc.wait_ge(w_in_in[0], 16)
                nc.scalar.activation(w_in_s[:, 0, HI, POOL_W:], w_in_stage[0][:, POOL_W:], ACT.Copy,
                                     scale=g1[:, 0:1]).then_inc(w_in_first_hi, 1)
                nc.scalar.activation(w_in_s[:, 0, HI, 0:POOL_W], w_in_stage[0][:, 0:POOL_W], ACT.Copy,
                                     scale=g1[:, 0:1]).then_inc(w_in_hi, 1)

            def split_w_in(k):
                sc.wait_ge(w_in_in[k % 6], 16 * (k // 6 + 1))
                nc.scalar.activation(w_in_s[:, k, HI, :], w_in_stage[k % 6], ACT.Copy,
                                     scale=g1[:, k:k + 1]).then_inc(w_in_hi, 1)

            def split_w_out(k):
                sc.wait_ge(in_done, KT * (NT - 1) + (2 * D * (k + 1) - 1) // (2 * IN_W) + 1)
                sc.wait_ge(w_out_in[W_OUT_SLOT[k]], w_out_count(k))
                nc.scalar.activation(w_out_s[:, k, HI, :], w_out_stage[W_OUT_SLOT[k]], ACT.Copy).then_inc(rows_hi, 1)

            def w_out_count(k):
                return sum(16 if j < KT // 2 else 32 for j in range(k + 1) if W_OUT_SLOT[j] == W_OUT_SLOT[k])

            def copy_kv(t):
                if t >= 1:
                    sc.wait_ge(values_ready, t)
                    sc.wait_ge(uT_done, t)
                    sc.wait_ge(kT_done, t)
                sc.wait_ge(kv_done, t + 1)
                sc.wait_ge(rinv_ready, t + 1)
                nc.scalar.activation(qkv[:, Q_W:Q_W + KV_W], bank[KV_B][:, 0:KV_W], ACT.Copy,
                                     scale=rinv[:, t:t + 1]).then_inc(kv_copied, 1)

            def copy_q(t):
                sc.wait_ge(q_done, t + 1)
                nc.scalar.activation(qkv[:, 0:Q_W].rearrange("p (t s d) -> p s t d", s=2, t=PAIRS),
                                     bank[Q_B][:, :].rearrange("p (s t d) -> p s t d", s=2, t=PAIRS),
                                     ACT.Copy, scale=rinv[:, t:t + 1]).then_inc(q_copied, 1)

            def copy_u(t):
                sc.wait_ge(in_done, KT * (t + 1))
                nc.scalar.activation(u_tok, bank[U_B][:, :], ACT.Copy, scale=rinv[:, t:t + 1]).then_inc(u_copied, 1)

            def evac_u(t):
                if t == 0:
                    sc.wait_ge(pads_ready, 1)
                sc.wait_ge(uT_done, t + 1)
                if t >= 1:
                    sc.wait_ge(pooled_ready, t)
                    sc.wait_ge(u_T_ready, t)
                    nc.scalar.activation(u_T[:, :, 0:HALO], u_T[:, :, P:P + HALO], ACT.Copy).then_inc(halo_ready, 1)
                    sc.wait_ge(halo_ready, t)
                nc.scalar.activation(u_T[:, :, HALO:UB], bank[UT_B][:, :].rearrange("p (g n) -> p g n", g=GROUPS),
                                     ACT.Copy).then_inc(u_T_ready, 1)

            def evac_qk(t):
                if t == 0:
                    sc.wait_ge(setup_done, 1)
                sc.wait_ge(qT_done, t + 1)
                src = bank[QT_B][:, :].rearrange("p (t c i) -> p c t i", t=PAIRS, c=2)
                for s in range(2):
                    half = slice(s * HD, (s + 1) * HD)
                    nc.scalar.activation(q_diag[half, :, :, half], src[half, :, :, :], ACT.Copy,
                                         scale=q_gain[half, :]).then_inc(q_diag_ready, 1)
                sc.wait_ge(kT_done, t + 1)
                nc.scalar.activation(keys_T[:, CHUNK + t * P:CHUNK + (t + 1) * P], bank[KT_B][:, 0:P], ACT.Copy,
                                     scale=k_gain).then_inc(keys_ready, 1)

            def evac_probs(t):
                for c in range(2):
                    n = 2 * t + c
                    sc.wait_ge(pT_done, n + 1)
                    if t >= 1:
                        sc.wait_ge(pv_done, n - 1)
                    nc.scalar.activation(probs_T[c], bank[SC_B[c]][:, :], ACT.Copy).then_inc(pT_copied, 1)

            def mix_high(t):
                sc.wait_ge(mix_done, t + 1)
                for g in range(GROUPS):
                    nc.scalar.activation(act[:, HI, g, tile(t)], bank[MIX_B][:, g * P:(g + 1) * P], ACT.Copy,
                                         scale=pool_sc[:, g:g + 1]).then_inc(mix_hi, 1)

            def attention_high(t):
                for c in range(2):
                    n = 2 * t + c
                    sc.wait_ge(pv_done, n + 1)
                    src = bank[OUT_B[c]][:, :].rearrange("p (t s i) -> p s t i", t=PAIRS, s=2)
                    tok = slice(n * CHUNK, (n + 1) * CHUNK)
                    for s in range(2):
                        half = slice(s * HD, (s + 1) * HD)
                        nc.scalar.activation(act[half, HI, 4:8, tok], src[half, s, :, :], ACT.Copy).then_inc(att_hi, 1)

            def exponentials(t, cs=(0, 1)):
                for c in cs:
                    n = 2 * t + c
                    sc.wait_ge(negmax_ready, n + 1)
                    for pr in range(PAIRS):
                        nc.scalar.activation(scores[c][:, pr, :], scores[c][:, pr, :], ACT.Exp,
                                             bias=neg_max[c][:, pr:pr + 1],
                                             accum_out=row_sum[c][:, pr:pr + 1]).then_inc(exp_done, 1)
                    sc.wait_ge(gap_ready, n + 1)
                    nc.scalar.activation(sink_exp[c], sink_gap[c], ACT.Exp).then_inc(exp_done, 1)

            def split_up(slot, U):
                sc.wait_ge(up_in[slot], U * 8 + (16, 8)[slot])
                nc.scalar.activation(up_s[slot][:, HI, :, :], up_stage[slot], ACT.Copy).then_inc(up_hi, 1)

            def split_down(c, dh):
                sc.wait_ge(down_in[dh], c * 16 + 16)
                nc.scalar.activation(down_s[dh][:, HI, :, :], down_stage[dh], ACT.Copy).then_inc(rows_hi, 1)

            sc.dma_start(gain_rows[0:KT, :], norm1_g[0].rearrange("(k p) -> k p", p=P)).then_inc(gain_rows_in, 16)
            sc.dma_start(gain_rows[KT:KT + GROUPS, :],
                         pool_scale[0].rearrange("(g p) -> g p", p=P)).then_inc(gain_rows_in, 16)
            xT_high(0)
            sc.wait_ge(gains_done, 1)
            nc.scalar.activation(gains, bank[GAIN_B][:, 0:KT + GROUPS], ACT.Copy).then_inc(gains_ready, 1)
            split_first_w_in()
            for k in range(1, KT):
                split_w_in(k)
            sum_squares_x(0)
            for t in range(NT):
                if t + 1 < NT:
                    xT_high(t + 1)
                if 1 <= t < NT - 1:
                    sum_squares_x(t + 1)
                if t == NT - 1:
                    split_w_out(0)
                    split_w_out(1)
                if t >= 1:
                    evac_u(t - 1)
                    evac_qk(t - 1)
                if t == NT - 1:
                    for k in range(2, 6):
                        split_w_out(k)
                copy_kv(t)
                copy_q(t)
                if t >= 2:
                    evac_probs(t - 2)
                copy_u(t)
                if t == 0:
                    sum_squares_x(1)
                if t >= 1:
                    mix_high(t - 1)
                if t >= 2:
                    attention_high(t - 2)
                if t >= 1:
                    exponentials(t - 1, (0,))
                if t == NT - 1:
                    split_w_out(6)
                    evac_u(t)
                if t >= 1:
                    exponentials(t - 1, (1,))
            evac_qk(NT - 1)
            split_w_out(KT - 1)
            evac_probs(NT - 2)
            mix_high(NT - 1)
            attention_high(NT - 2)
            exponentials(NT - 1)
            sum_squares_x1(0)
            evac_probs(NT - 1)
            sum_squares_x1(1)
            attention_high(NT - 1)
            for t in range(2, NT):
                xT_high(NT + t - 2)
                sum_squares_x1(t)
                if t == 3:
                    split_up(0, 0)
                    split_up(1, 1)
            xT_high(2 * NT - 2)

            def chunk(c, first=False, last=False):
                for n, (f, h) in enumerate(ORDER):
                    N = c * NZ + n
                    if first and n == 1:
                        xT_high(2 * NT - 1)
                    sc.wait_ge(z_done, N + 1)
                    if not (first and n < 2):
                        sc.wait_ge(hid_lo, N - 1)
                    nc.scalar.activation(relu_buf[n % 2], bank[Z_B[n % 2]][:, :], ACT.Relu).then_inc(relu_done, 1)
                    sc.wait_ge(relu_done, N + 1)
                    nc.scalar.activation(relu_buf[n % 2], relu_buf[n % 2], ACT.Square).then_inc(sq_done, 1)
                    sc.wait_ge(sq_done, N + 1)
                    nc.scalar.activation(hid[:, f, HI, h * HALF:(h + 1) * HALF], relu_buf[n % 2],
                                         ACT.Copy).then_inc(hid_hi, 1)
                    if n in (2, 3):
                        split_up(n - 2, c * FC + n)
                    elif n in (4, 5):
                        split_down(c, n - 4)
                if not last:
                    split_up(0, (c + 1) * FC)
                    split_up(1, (c + 1) * FC + 1)

            chunk(0, first=True)
            with sc.Fori(1, NC_FF - 1) as c:
                chunk(c)
            chunk(NC_FF - 1, last=True)

        @block.vector
        def _(dve):
            def xT_low(T):
                t = T % NT
                for i in range(2):
                    dve.wait_ge(xT_hi, 2 * T + i + 1)
                    src = bank[XT_B[T // NT][i]][:, :].rearrange("p (k n) -> p k n", k=4)
                    nc.vector.tensor_tensor(out=act[:, LO, 4 * i:4 * i + 4, tile(t)], in0=src,
                                            in1=act_f[:, HI, 4 * i:4 * i + 4, tile(t)],
                                            op=ALU.subtract).then_inc(xT_lo, 1)

            def normed_x1(t):
                T = NT + t
                dve.wait_ge(rinv_ready, T + 1)
                dve.wait_ge(xT_done, 2 * T)
                dve.wait_ge(tok_added, 2 * t + 2)
                if t == 0:
                    dve.wait_ge(norm2_in, 16)
                nc.vector.scalar_tensor_tensor(out=x_norm, in0=resid[t], scalar=rinv[:, T:T + 1], in1=norm2_row,
                                               op0=ALU.mult, op1=ALU.mult).then_inc(x_norm_ready, 1)

            def split_first_w_in():
                dve.wait_ge(gains_ready, 1)
                for cols, src_ready, done in ((slice(POOL_W, IN_W), w_in_first_hi, w_in_first_lo),
                                              (slice(0, POOL_W), w_in_hi, w_in_lo)):
                    dve.wait_ge(src_ready, 1)
                    nc.vector.scalar_tensor_tensor(out=w_in_s[:, 0, LO, cols], in0=w_in_stage[0][:, cols],
                                                   scalar=g1[:, 0:1], in1=w_in_s[:, 0, HI, cols].bitcast(F32),
                                                   op0=ALU.mult, op1=ALU.subtract).then_inc(done, 1)

            def split_w_in(k):
                dve.wait_ge(w_in_hi, k + 1)
                nc.vector.scalar_tensor_tensor(out=w_in_s[:, k, LO, :], in0=w_in_stage[k % 6], scalar=g1[:, k:k + 1],
                                               in1=w_in_s[:, k, HI, :].bitcast(F32), op0=ALU.mult,
                                               op1=ALU.subtract).then_inc(w_in_lo, 1)

            def split_w_out(k):
                dve.wait_ge(rows_hi, k + 1)
                nc.vector.tensor_tensor(out=w_out_s[:, k, LO, :], in0=w_out_stage[W_OUT_SLOT[k]],
                                        in1=w_out_s[:, k, HI, :].bitcast(F32), op=ALU.subtract).then_inc(rows_lo, 1)

            def pooled(t):
                dve.wait_ge(win_step, 4 * t + 4)
                sums = [win_a[:, 0, :], win_b[:, 0, :], win_a[:, 2, :], win_b[:, 2, :]]
                if t == 0:
                    for g in range(GROUPS):
                        nc.vector.tensor_tensor(out=sums[g][:, HALO:2 * HALO], in0=sums[g][:, HALO:2 * HALO],
                                                in1=edge[:, g, :], op=ALU.mult).then_inc(pool_step, 1)
                    dve.wait_ge(pool_step, GROUPS)
                for g in range(GROUPS):
                    nc.vector.scalar_tensor_tensor(out=sums[g][:, HALO:UB], in0=sums[g][:, HALO:UB],
                                                   scalar=1.0 / WINDOWS[g], in1=u_T[:, g, HALO:UB],
                                                   op0=ALU.mult, op1=ALU.subtract).then_inc(
                                                       pooled_ready if g == GROUPS - 1 else pool_step, 1)

            def place_values(t):
                dve.wait_ge(kv_copied, t + 1)
                v = qkv[:, Q_W + P:Q_W + KV_W]
                nc.vector.tensor_copy(values[:, t % 4, 1, :], v)
                nc.vector.tensor_copy(values[HD:P, t % 4, 0, :], v[0:HD, :])
                nc.vector.tensor_copy(values[0:HD, (t + 1) % 4, 0, :], v[HD:P, :]).then_inc(values_ready, 1)

            def head_sums(t):
                dve.wait_ge(squares_ready, t + 1)
                nc.vector.reduce_sum(h_ssq, squares.rearrange("p (h d) -> p h d", d=HD), axis=AX.X).then_inc(h_ssq_ready, 1)

            def head_norm(t):
                dve.wait_ge(h_rinv_ready, t + 1)
                qk = qkv[:, 0:Q_W + P].rearrange("p (h d) -> p h d", d=HD)
                scale = h_rinv.rearrange("p (h a) -> p h a", a=1).to_broadcast([P, NH, HD])
                nc.vector.tensor_tensor(out=qk, in0=qk, in1=scale, op=ALU.mult).then_inc(qk_ready, 1)

            def softmax_head(t, cs=(0, 1)):
                for c in cs:
                    n = 2 * t + c
                    dve.wait_ge(scores_done, n + 1)
                    src = bank[SC_B[c]][:, :].rearrange("p (t j) -> p t j", t=PAIRS)
                    lo = CHUNK if n == 0 else 0
                    nc.vector.tensor_tensor(out=scores[c][:, :, lo:], in0=src[:, :, lo:], in1=bias[:, :, lo:],
                                            op=ALU.add).then_inc(biased, 1)
                    dve.wait_ge(biased, n + 1)
                    nc.vector.reduce_max(smax[c], scores[c], axis=AX.X).then_inc(max_ready, 1)
                    dve.wait_ge(max_ready, n + 1)
                    nc.vector.scalar_tensor_tensor(out=neg_max[c], in0=smax[c], scalar=-1.0, in1=neg_sink,
                                                   op0=ALU.mult, op1=ALU.min).then_inc(negmax_ready, 1)
                    dve.wait_ge(negmax_ready, n + 1)
                    nc.vector.tensor_tensor(out=sink_gap[c], in0=neg_max[c], in1=neg_sink,
                                            op=ALU.subtract).then_inc(gap_ready, 1)

            def softmax_tail(t):
                for c in range(2):
                    n = 2 * t + c
                    dve.wait_ge(exp_done, (PAIRS + 1) * (n + 1))
                    nc.vector.tensor_tensor(out=denom[c], in0=row_sum[c], in1=sink_exp[c],
                                            op=ALU.add).then_inc(denom_ready, 1)
                    dve.wait_ge(denom_ready, n + 1)
                    nc.vector.reciprocal(inv_den[c], denom[c]).then_inc(inv_ready, 1)
                    dve.wait_ge(inv_ready, n + 1)
                    for pr in range(PAIRS):
                        nc.vector.tensor_scalar(out=scores[c][:, pr, :], in0=scores[c][:, pr, :],
                                                scalar1=inv_den[c][:, pr:pr + 1], scalar2=None,
                                                op0=ALU.mult).then_inc(probs_ready, 1)

            def mix_low(t):
                dve.wait_ge(mix_hi, GROUPS * (t + 1))
                for g in range(GROUPS):
                    nc.vector.scalar_tensor_tensor(out=act[:, LO, g, tile(t)], in0=bank[MIX_B][:, g * P:(g + 1) * P],
                                                   scalar=pool_sc[:, g:g + 1], in1=act_f[:, HI, g, tile(t)],
                                                   op0=ALU.mult, op1=ALU.subtract).then_inc(mix_lo, 1)

            def attention_low(t):
                for c in range(2):
                    n = 2 * t + c
                    src = bank[OUT_B[c]][:, :].rearrange("p (t s i) -> p s t i", t=PAIRS, s=2)
                    tok = slice(n * CHUNK, (n + 1) * CHUNK)
                    for s in range(2):
                        dve.wait_ge(att_hi, 2 * n + s + 1)
                        half = slice(s * HD, (s + 1) * HD)
                        nc.vector.tensor_tensor(out=act[half, LO, 4:8, tok], in0=src[half, s, :, :],
                                                in1=act_f[half, HI, 4:8, tok], op=ALU.subtract).then_inc(att_lo, 1)

            def add_out(G, bank_of_out, t, dh):
                dve.wait_ge(tok_done, G + 1)
                dst = resid[t][:, dh * BANK:(dh + 1) * BANK]
                nc.vector.tensor_tensor(out=dst, in0=bank_of_out[:, :], in1=dst, op=ALU.add).then_inc(tok_added, 1)

            def add_x1(t):
                dve.wait_ge(resid_in[t], 16)
                for dh in range(2):
                    add_out(2 * t + dh, bank[TOK_B[(2 * t + dh) % 4]], t, dh)

            def split_up(slot, U):
                dve.wait_ge(up_hi, U + 1)
                nc.vector.tensor_tensor(out=up_s[slot][:, LO, :, :], in0=up_stage[slot],
                                        in1=up_s[slot][:, HI, :, :].bitcast(F32), op=ALU.subtract).then_inc(up_lo, 1)

            def split_down(c, dh):
                dve.wait_ge(rows_hi, c * 2 + KT + dh + 1)
                nc.vector.tensor_tensor(out=down_s[dh][:, LO, :, :], in0=down_stage[dh],
                                        in1=down_s[dh][:, HI, :, :].bitcast(F32), op=ALU.subtract).then_inc(rows_lo, 1)

            dve.wait_ge(setup_pool, 6)
            steps = [0]

            def step(ins):
                steps[0] += 1
                ins.then_inc(setup_dve, 1)
                dve.wait_ge(setup_dve, steps[0])

            step(nc.vector.scalar_tensor_tensor(out=dist, in0=dist, scalar=-1.0, in1=dist, op0=ALU.mult, op1=ALU.max))
            for pr in range(PAIRS):
                for s in range(2):
                    half = slice(s * HD, (s + 1) * HD)
                    slope = 2.0 ** (-8.0 * (pr + s * PAIRS + 1) / NQ)
                    step(nc.vector.tensor_scalar(out=bias[half, pr, :], in0=dist[half, :], scalar1=-slope,
                                                 scalar2=None, op0=ALU.mult))

            def window_edges():
                for g, w in enumerate(WINDOWS):
                    step(nc.vector.tensor_scalar(out=edge[:, g, :], in0=edge[:, g, :], scalar1=float(w), scalar2=None,
                                                 op0=ALU.min))
                step(nc.vector.reciprocal(edge, edge))
                for g, w in enumerate(WINDOWS):
                    step(nc.vector.tensor_scalar(out=edge[:, g, :], in0=edge[:, g, :], scalar1=float(w), scalar2=None,
                                                 op0=ALU.mult))

            xT_low(0)
            split_first_w_in()
            for k in range(1, KT):
                split_w_in(k)
            xT_low(1)
            dve.wait_ge(w_in_lo, KT)
            nc.vector.memset(keys_T[:, 0:CHUNK], 0.0).then_inc(zeroed, 1)
            nc.vector.memset(q_diag, 0.0).then_inc(zeroed, 1)
            nc.vector.memset(u_T[:, :, 0:HALO], 0.0).then_inc(zeroed, 1)
            nc.vector.memset(values[0:HD, 0, 0, :], 0.0).then_inc(zeroed, 1)
            dve.wait_ge(zeroed, 4)
            nc.vector.memset(scores[0][:, :, 0:CHUNK], MASK).then_inc(pads_ready, 1)
            dve.wait_ge(pads_ready, 1)
            dve.wait_ge(consts_in, 16 * N_CONST)
            step(nc.vector.tensor_scalar(out=q_gain, in0=q_gain, scalar1=HD ** -0.5, scalar2=None, op0=ALU.mult))
            nc.vector.tensor_scalar(out=neg_sink, in0=neg_sink, scalar1=-1.0, scalar2=None,
                                    op0=ALU.mult).then_inc(setup_done, 1)
            dve.wait_ge(setup_done, 1)

            for t in range(NT):
                if 1 <= t < NT - 1:
                    xT_low(t + 1)
                if t == 1:
                    window_edges()
                if t == NT - 1:
                    for k in range(4):
                        split_w_out(k)
                if t >= 1:
                    pooled(t - 1)
                if t == NT - 1:
                    split_w_out(4)
                place_values(t)
                head_sums(t)
                if t == NT - 1:
                    split_w_out(5)
                if t >= 1:
                    softmax_head(t - 1, (0,))
                    mix_low(t - 1)
                if t >= 2:
                    attention_low(t - 2)
                if t == NT - 1:
                    head_norm(t)
                if t >= 1:
                    softmax_head(t - 1, (1,))
                if t < NT - 1:
                    head_norm(t)
                if t == NT - 1:
                    split_w_out(6)
                if t >= 1:
                    softmax_tail(t - 1)
            pooled(NT - 1)
            split_w_out(7)
            mix_low(NT - 1)
            softmax_head(NT - 1)
            attention_low(NT - 2)
            softmax_tail(NT - 1)
            add_x1(0)
            normed_x1(0)
            add_x1(1)
            attention_low(NT - 1)
            for t in range(2, NT):
                xT_low(NT + t - 2)
                normed_x1(t - 1)
                add_x1(t)
                if t == 3:
                    split_up(0, 0)
                    split_up(1, 1)
            xT_low(2 * NT - 2)
            normed_x1(NT - 1)

            def chunk(c, first=False, last=False):
                for n, (f, h) in enumerate(ORDER):
                    if first and n == 1:
                        xT_low(2 * NT - 1)
                    dve.wait_ge(hid_hi, c * NZ + n + 1)
                    half = slice(h * HALF, (h + 1) * HALF)
                    nc.vector.tensor_tensor(out=hid[:, f, LO, half], in0=relu_buf[n % 2],
                                            in1=hid[:, f, HI, half].bitcast(F32), op=ALU.subtract).then_inc(hid_lo, 1)
                    if n in (2, 3):
                        split_up(n - 2, c * FC + n)
                    elif n in (4, 5):
                        split_down(c, n - 4)
                if not last:
                    split_up(0, (c + 1) * FC)
                    split_up(1, (c + 1) * FC + 1)
                for dh in range(2):
                    for t in range(NT):
                        G = (c + 1) * NTOK + dh * NT + t
                        dve.wait_ge(tok_added, G - NTOK + 1)
                        add_out(G, bank[TOK_B[(dh * NT + t) % 4]], t, dh)

            chunk(0, first=True)
            with dve.Fori(1, NC_FF - 1) as c:
                chunk(c)
            chunk(NC_FF - 1, last=True)

        @block.tensor
        def _(pe):
            def passes(out_ap, lhs, rhs, first, last):
                nc.tensor.matmul(out_ap, lhs[HI], rhs[HI], start=first, stop=False)
                nc.tensor.matmul(out_ap, lhs[HI], rhs[LO], start=False, stop=False)
                return nc.tensor.matmul(out_ap, lhs[LO], rhs[HI], start=False, stop=last)

            def transpose_x(T):
                stage = T // NT
                src = x_slot[T % 2] if stage == 0 else x_norm
                if stage == 0:
                    pe.wait_ge(x_in[T % 2], 16 * (T // 2 + 1))
                else:
                    pe.wait_ge(x_norm_ready, T - NT + 1)
                if stage == 0 and T >= 3:
                    pe.wait_ge(mix_lo, GROUPS * (T - 2))
                    if T >= 4:
                        pe.wait_ge(att_lo, 4 * (T - 3))
                if T >= 1:
                    pe.wait_ge(xT_lo, 2 * T)
                for i in range(2):
                    for k in range(4):
                        last = nc.tensor.transpose(bank[XT_B[stage][i]][:, k * P:(k + 1) * P],
                                                   src[:, (4 * i + k) * P:(4 * i + k + 1) * P], ident)
                    last.then_inc(xT_done, 1)

            def project_in(t, ks):
                lhs = lambda k: [act[:, part, k, tile(t)] for part in (HI, LO)]
                rhs = lambda k, a, n: [w_in_s[:, k, part, a:a + n] for part in (HI, LO)]
                for k in ks:
                    if k in (0, KT // 2):
                        pe.wait_ge(xT_lo, 2 * t + (1 if k == 0 else 2))
                    if t == 0 and k == 0:
                        pe.wait_ge(w_in_first_lo, 1)
                    elif t == 0:
                        pe.wait_ge(w_in_lo, k + 1)
                    first, stop = k == 0, k == KT - 1
                    if k == 0 and t >= 1:
                        pe.wait_ge(kv_copied, t)
                    last = passes(bank[KV_B][:, 0:KV_W], lhs(k), rhs(k, POOL_W + Q_W, KV_W), first, stop)
                    if stop:
                        last.then_inc(kv_done, 1)
                    if k == 0 and t >= 1:
                        pe.wait_ge(q_copied, t)
                    last = passes(bank[Q_B][:, :], lhs(k), rhs(k, POOL_W, Q_W), first, stop)
                    if stop:
                        last.then_inc(q_done, 1)
                    if k == 0 and t == 0:
                        pe.wait_ge(w_in_lo, 1)
                    elif k == 0:
                        pe.wait_ge(u_copied, t)
                    last = passes(bank[U_B][:, :], lhs(k), rhs(k, 0, POOL_W), first, stop)
                    last.then_inc(in_done, 1)

            def project_out(t, ks):
                for k in ks:
                    if k == 0:
                        for dh in range(2):
                            if 2 * t + dh >= 4:
                                pe.wait_ge(tok_added, 2 * t + dh - 3)
                        if t == 0:
                            pe.wait_ge(kv_copied, NT)
                            pe.wait_ge(q_copied, NT)
                        if t == 1:
                            pe.wait_ge(u_copied, NT)
                            pe.wait_ge(mix_lo, GROUPS * NT)
                        if t == NT - 1:
                            pe.wait_ge(mix_lo, GROUPS * NT)
                    if k == KT // 2:
                        pe.wait_ge(att_lo, 4 * (t + 1))
                    if t == 0:
                        pe.wait_ge(rows_lo, k + 1)
                    for dh in range(2):
                        cols = slice(dh * BANK, (dh + 1) * BANK)
                        last = passes(bank[TOK_B[(2 * t + dh) % 4]][:, :],
                                      [act[:, part, k, tile(t)] for part in (HI, LO)],
                                      [w_out_s[:, k, part, cols] for part in (HI, LO)], k == 0, k == KT - 1)
                        if k == KT - 1:
                            last.then_inc(tok_done, 1)

            def transpose_in(t):
                pe.wait_ge(u_copied, t + 1)
                if t + 2 < NT:
                    pe.wait_ge(xT_lo, 2 * (t + 3))
                else:
                    pe.wait_ge(mix_lo, GROUPS * t)
                    pe.wait_ge(att_lo, 4 * (t - 1))
                for g in range(GROUPS):
                    last = nc.tensor.transpose(bank[UT_B][:, g * P:(g + 1) * P], u_tok[:, g * P:(g + 1) * P], ident)
                last.then_inc(uT_done, 1)
                pe.wait_ge(qk_ready, t + 1)
                for pr in range(PAIRS):
                    last = nc.tensor.transpose(bank[QT_B][:, pr * P:(pr + 1) * P], qkv[:, pr * P:(pr + 1) * P], ident)
                last.then_inc(qT_done, 1)
                if t >= 2:
                    pe.wait_ge(att_lo, 4 * (t - 1))
                nc.tensor.transpose(bank[KT_B][:, 0:P], qkv[:, Q_W:Q_W + P], ident).then_inc(kT_done, 1)

            def transpose_probs(t):
                for c in range(2):
                    pe.wait_ge(probs_ready, PAIRS * (2 * t + c + 1))
                    for pr in range(PAIRS):
                        last = nc.tensor.transpose(bank[SC_B[c]][:, pr * P:(pr + 1) * P], scores[c][:, pr, :], ident)
                    last.then_inc(pT_done, 1)

            def mix(t):
                pe.wait_ge(pooled_ready, t + 1)
                pe.wait_ge(u_T_ready, t + 1)
                windows = [win_a[:, 0, :], win_b[:, 0, :], win_a[:, 2, :], win_b[:, 2, :]]
                for g in range(GROUPS):
                    last = nc.tensor.matmul(bank[MIX_B][:, g * P:(g + 1) * P], pool_map[:, g, :],
                                            windows[g][:, HALO:UB], start=True, stop=True)
                last.then_inc(mix_done, 1)

            def score(t):
                pe.wait_ge(q_diag_ready, 2 * (t + 1))
                pe.wait_ge(keys_ready, t + 1)
                for c in range(2):
                    n = 2 * t + c
                    if t >= 1:
                        pe.wait_ge(pT_copied, n - 1)
                    for pr in range(PAIRS):
                        last = nc.tensor.matmul(bank[SC_B[c]][:, pr * P:(pr + 1) * P], q_diag[:, c, pr, :],
                                                keys_T[:, n * CHUNK:(n + 2) * CHUNK], start=True, stop=True)
                    last.then_inc(scores_done, 1)

            def attend(t):
                pe.wait_ge(values_ready, t + 1)
                if t + 1 < NT:
                    pe.wait_ge(q_diag_ready, 2 * (t + 2))
                    pe.wait_ge(keys_ready, t + 2)
                for c in range(2):
                    n = 2 * t + c
                    pe.wait_ge(pT_copied, n + 1)
                    nc.tensor.matmul(bank[OUT_B[c]][:, :], values[:, t % 4, c, :], probs_T[c],
                                     start=True, stop=True).then_inc(pv_done, 1)

            pe.wait_ge(setup_pool, 6)
            transpose_x(0)
            pe.wait_ge(gain_rows_in, 32)
            nc.tensor.transpose(bank[GAIN_B][:, 0:KT + GROUPS], gain_rows,
                                ident[0:KT + GROUPS, 0:KT + GROUPS]).then_inc(gains_done, 1)
            for t in range(NT):
                a, b = {0: (7, 7), 1: (1, 4), NT - 1: (2, 4)}.get(t, (2, 5))
                project_in(t, range(0, a))
                if t + 1 < NT:
                    transpose_x(t + 1)
                project_in(t, range(a, b))
                if t >= 1:
                    transpose_in(t - 1)
                project_in(t, range(b, KT))
                if t >= 2:
                    transpose_probs(t - 2)
                if t >= 1:
                    mix(t - 1)
                    score(t - 1)
                if t >= 2:
                    attend(t - 2)
            project_out(0, range(0, 3))
            transpose_in(NT - 1)
            project_out(0, range(3, 7))
            transpose_probs(NT - 2)
            mix(NT - 1)
            score(NT - 1)
            attend(NT - 2)
            project_out(0, range(7, KT))
            project_out(1, range(KT))
            transpose_probs(NT - 1)
            project_out(2, range(0, 3))
            attend(NT - 1)
            transpose_x(NT)
            project_out(2, range(3, KT))
            for t in range(3, NT):
                transpose_x(NT + t - 2)
                project_out(t, range(KT))
            transpose_x(2 * NT - 2)

            def hidden(c, n, first):
                f, h = ORDER[n]
                slot = f % 2
                if h == 0:
                    pe.wait_ge(up_lo, c * FC + f + 1)
                if first and n == 0:
                    pe.wait_ge(att_lo, 4 * NT)
                if first and n < 4:
                    pe.wait_ge(xT_lo, 2 * (NT + NT // 2 * (h + 1)))
                if not (first and n < 2):
                    pe.wait_ge(relu_done, c * NZ + n - 1)
                half = slice(h * HALF, (h + 1) * HALF)
                for k in range(KT):
                    last = passes(bank[Z_B[n % 2]][:, :], [up_s[slot][:, part, k, :] for part in (HI, LO)],
                                  [act[:, part, k, half] for part in (HI, LO)], k == 0, k == KT - 1)
                last.then_inc(z_done, 1)

            def down(c):
                for dh in range(2):
                    pe.wait_ge(rows_lo, c * 2 + KT + dh + 1)
                    for t in range(NT):
                        g = dh * NT + t
                        pe.wait_ge(tok_added, (c + 1) * NTOK + g - 3)
                        if t % (NT // 2) == 0 and dh == 0:
                            pe.wait_ge(hid_lo, c * NZ + (NZ - 2 if t == 0 else NZ))
                        for f in range(FC):
                            last = passes(bank[TOK_B[g % 4]][:, :], [hid[:, f, part, tile(t)] for part in (HI, LO)],
                                          [down_s[dh][:, part, f, :] for part in (HI, LO)], f == 0, f == FC - 1)
                        last.then_inc(tok_done, 1)

            hidden(0, 0, True)
            transpose_x(2 * NT - 1)
            for n in range(1, NZ):
                hidden(0, n, True)
            down(0)
            with pe.Fori(1, NC_FF) as c:
                for n in range(NZ):
                    hidden(c, n, False)
                down(c)


_INS = ["x", "norm1_g", "w_in", "pool_w", "pool_scale", "q_norm_g", "k_norm_g", "sinks",
        "w_out", "norm2_g", "w_up", "w_down"]


def kernel(**inputs):
    import numpy as np
    import concourse.bacc as bacc
    from concourse.bass_utils import run_bass_kernel_spmd

    nc = bacc.Bacc("TRN2", target_bir_lowering=False, num_devices=1)
    arrays, args = {}, []
    for name in _INS:
        a = np.ascontiguousarray(inputs[name])
        arrays[f"in_{name}"] = a
        args.append(nc.dram_tensor(f"in_{name}", a.shape, mybir.dt.from_np(a.dtype), kind="ExternalInput").ap())
    shape = arrays["in_x"].shape
    args.append(nc.dram_tensor("out_x", shape, F32, kind="ExternalOutput").ap())
    hybrid_trunk(nc, *args)
    result = run_bass_kernel_spmd(nc, [arrays], core_ids=[0])
    return result.results[0]["out_x"]
```
